# Optimizing a Trainium2 kernel written in Bass

```python
import jax, jax.numpy as jnp
from jax import lax
import numpy as np

D_MODEL = 1024
BATCH = 1
SEQ = 1024
DEPTH = 1
DEC_BATCH = 8
DEC_SEQ = 1
PAST_LEN = 8192
PAGE_SIZE = 128

HGRN_HEADS = 4
HGRN_DK = 128
HGRN_DV = 128
HGRN_KEY_WIDTH = HGRN_HEADS * HGRN_DK
HGRN_VAL_WIDTH = HGRN_HEADS * HGRN_DV
CHUNK = 32
CONV_WIDTH = 512
CONV_K = 3
IN_WIDTH = 2 * HGRN_KEY_WIDTH + 2 * HGRN_VAL_WIDTH + 3 * CONV_WIDTH + 2 * D_MODEL
N_EXPERTS = 64
TOP_K = 8
N_GROUPS = 8
TOPK_GROUPS = 4
EXPERT_FF = 256
SHARED_FF = 256
ROUTED_SCALE = 2.5
MOE_BLOCK = 128
NORM_EPS = 1e-6

kernel_name = "hgrn2_shortconv_moe_adaln_decode_step"

def _split_points():
    sizes = (HGRN_KEY_WIDTH, HGRN_KEY_WIDTH, HGRN_VAL_WIDTH, HGRN_VAL_WIDTH,
             CONV_WIDTH, CONV_WIDTH, CONV_WIDTH, D_MODEL, D_MODEL)
    return list(np.cumsum(sizes)[:-1])

def rmsnorm(x, g):
    xf = x.astype(jnp.float32)
    y = xf * lax.rsqrt(jnp.mean(xf * xf, axis=-1, keepdims=True) + NORM_EPS)
    return (y * g.astype(jnp.float32)).astype(x.dtype)

def swiglu(x, w_gate, w_up, w_down):
    return (jax.nn.silu(x @ w_gate) * (x @ w_up)) @ w_down

def hgrn2_chunked(q, k, v, log_f, s0):
    B, T, H, _ = q.shape
    pad = (-T) % CHUNK
    n_chunks = (T + pad) // CHUNK

    def to_chunks(a):
        a = jnp.pad(a, ((0, 0), (0, pad), (0, 0), (0, 0)))
        return a.reshape(B, n_chunks, CHUNK, H, a.shape[-1]).transpose(1, 0, 3, 2, 4)

    q, k, v, log_f = (to_chunks(a) for a in (q, k, v, log_f))
    b = jnp.cumsum(log_f, axis=3)
    b_last = b[:, :, :, -1:, :]
    q_in = q * jnp.exp(b)
    k_in = k * jnp.exp(-b)
    k_end = k * jnp.exp(b_last - b)
    causal = jnp.tril(jnp.ones((CHUNK, CHUNK), dtype=bool))
    att = jnp.where(causal, jnp.einsum("nbhtd,nbhsd->nbhts", q_in, k_in), 0.0)
    o_intra = jnp.einsum("nbhts,nbhsv->nbhtv", att, v)

    def step(S, xs):
        q_c, k_c, v_c, decay = xs
        o_c = jnp.einsum("bhtd,bhdv->bhtv", q_c, S)
        S = decay[..., None] * S + jnp.einsum("bhsd,bhsv->bhdv", k_c, v_c)
        return S, o_c

    s_fin, o_inter = lax.scan(step, s0, (q_in, k_end, v, jnp.exp(b_last[:, :, :, 0, :])))
    o = (o_intra + o_inter).transpose(1, 0, 3, 2, 4).reshape(B, n_chunks * CHUNK, H, -1)[:, :T]
    return o, s_fin

def hgrn2_branch(q_raw, f_raw, i_raw, g_raw, s0, lb, head_g):
    B, T, _ = q_raw.shape
    split_heads = lambda a, d: a.astype(jnp.float32).reshape(B, T, HGRN_HEADS, d)
    lb_h = lb.reshape(HGRN_HEADS, HGRN_DK)
    f = lb_h + (1.0 - lb_h) * jax.nn.sigmoid(split_heads(f_raw, HGRN_DK))
    q = jax.nn.silu(split_heads(q_raw, HGRN_DK))
    o, s_new = hgrn2_chunked(q, 1.0 - f, split_heads(i_raw, HGRN_DV), jnp.log(f), s0.astype(jnp.float32))
    o = rmsnorm(o, head_g) * jax.nn.silu(split_heads(g_raw, HGRN_DV))
    return o.reshape(B, T, HGRN_VAL_WIDTH).astype(q_raw.dtype), s_new.astype(s0.dtype)

def short_conv_branch(b_gate, c_gate, v, buf0, w_conv, b_conv):
    u = c_gate * v
    buf = jnp.concatenate([buf0.astype(u.dtype), u], axis=1)
    T = u.shape[1]
    conv = sum((buf[:, j:j + T] * w_conv[j] for j in range(CONV_K)), b_conv)
    return b_gate * conv, buf[:, T:]

def route(h, w_router, router_bias):
    T = h.shape[0]
    scores = jax.nn.sigmoid((h @ w_router).astype(jnp.float32))
    sel = scores + router_bias.astype(jnp.float32)
    grp = sel.reshape(T, N_GROUPS, N_EXPERTS // N_GROUPS)
    grp_score = lax.top_k(grp, 2)[0].sum(-1)
    _, top_g = lax.top_k(grp_score, TOPK_GROUPS)
    gmask = jax.nn.one_hot(top_g, N_GROUPS, dtype=jnp.float32).sum(1)
    emask = jnp.repeat(gmask, N_EXPERTS // N_GROUPS, axis=1) > 0
    _, top_i = lax.top_k(jnp.where(emask, sel, -jnp.inf), TOP_K)
    w = jnp.take_along_axis(scores, top_i, axis=1)
    w = w / jnp.sum(w, axis=-1, keepdims=True) * ROUTED_SCALE
    return top_i, w.astype(h.dtype)

def routed_experts(h, top_i, top_w, w_gate, w_up, w_down):
    T, D = h.shape
    A = T * TOP_K
    n_blocks = (A + N_EXPERTS * (MOE_BLOCK - 1)) // MOE_BLOCK
    n_rows = n_blocks * MOE_BLOCK
    e_flat = top_i.reshape(A).astype(jnp.int32)
    tok_flat = jnp.repeat(jnp.arange(T, dtype=jnp.int32), TOP_K)
    w_flat = top_w.reshape(A)
    order = jnp.argsort(e_flat)
    e_sorted = e_flat[order]
    counts = jnp.bincount(e_flat, length=N_EXPERTS).astype(jnp.int32)
    padded = (counts + MOE_BLOCK - 1) // MOE_BLOCK * MOE_BLOCK
    pad_end = jnp.cumsum(padded)
    pad_start = pad_end - padded
    start = jnp.cumsum(counts) - counts
    dest = pad_start[e_sorted] + jnp.arange(A, dtype=jnp.int32) - start[e_sorted]
    row_tok = jnp.full((n_rows,), T, jnp.int32).at[dest].set(tok_flat[order])
    row_w = jnp.zeros((n_rows,), h.dtype).at[dest].set(w_flat[order])
    blk_exp = jnp.minimum(
        jnp.searchsorted(pad_end, jnp.arange(n_blocks, dtype=jnp.int32) * MOE_BLOCK, side="right"),
        N_EXPERTS - 1)
    h_pad = jnp.concatenate([h, jnp.zeros((1, D), h.dtype)], axis=0)

    def block(args):
        tok, e = args
        return swiglu(h_pad[tok], w_gate[e], w_up[e], w_down[e])

    out = lax.map(block, (row_tok.reshape(n_blocks, MOE_BLOCK), blk_exp))
    out = out.reshape(n_rows, D) * row_w[:, None]
    return jax.ops.segment_sum(out, row_tok, num_segments=T + 1)[:T]

def layer(x, c, s_hgrn, s_conv, lb, p):
    B, T, D = x.shape
    mod = jax.nn.silu(c) @ p["w_ada"] + p["b_ada"]
    sh1, sc1, g1, sh2, sc2, g2 = [m[:, None, :] for m in jnp.split(mod, 6, axis=-1)]
    h = rmsnorm(x, p["norm_mix_g"]) * (1.0 + sc1) + sh1
    proj = h @ p["w_in"]
    qa, fa, ia, ga, bb, cc, vb, mga, mgb = jnp.split(proj, _split_points(), axis=-1)
    ya, s_hgrn_new = hgrn2_branch(qa, fa, ia, ga, s_hgrn, lb, p["hgrn_norm_g"])
    yb, s_conv_new = short_conv_branch(bb, cc, vb, s_conv, p["conv_w"], p["conv_b"])
    mixed = (jax.nn.sigmoid(mga) * (ya @ p["w_out_hgrn"])
             + jax.nn.sigmoid(mgb) * (yb @ p["w_out_conv"]))
    x = x + g1 * (mixed @ p["w_o"])
    h2 = (rmsnorm(x, p["norm_ffn_g"]) * (1.0 + sc2) + sh2).reshape(B * T, D)
    top_i, top_w = route(h2, p["w_router"], p["router_bias"])
    ffn = (routed_experts(h2, top_i, top_w, p["w_exp_gate"], p["w_exp_up"], p["w_exp_down"])
           + swiglu(h2, p["w_sh_gate"], p["w_sh_up"], p["w_sh_down"]))
    x = x + g2 * ffn.reshape(B, T, D)
    return x, s_hgrn_new, s_conv_new

def setup_inputs(seed: int = 0) -> dict:
    key = jax.random.key(seed)
    ks = jax.random.split(key, 32)
    nrm = lambda k, shape, scale: jax.random.normal(k, shape, jnp.float32) * scale
    D = D_MODEL
    return {
        "x_prompt": nrm(ks[0], (BATCH, SEQ, D), 1.0),
        "x_sample": nrm(ks[1], (DEC_BATCH, DEC_SEQ, D), 1.0),
        "state_hgrn": nrm(ks[2], (DEPTH, DEC_BATCH, HGRN_HEADS, HGRN_DK, HGRN_DV), 0.3),
        "state_conv": nrm(ks[3], (DEPTH, DEC_BATCH, CONV_K - 1, CONV_WIDTH), 1.0),
        "c_prompt": nrm(ks[4], (BATCH, D), 1.0),
        "c_sample": nrm(ks[5], (DEC_BATCH, D), 1.0),
        "w_ada": nrm(ks[6], (DEPTH, D, 6 * D), 0.5 * D ** -0.5),
        "b_ada": nrm(ks[7], (DEPTH, 6 * D), 0.02),
        "norm_mix_g": 1.0 + nrm(ks[8], (DEPTH, D), 0.02),
        "norm_ffn_g": 1.0 + nrm(ks[9], (DEPTH, D), 0.02),
        "w_in": nrm(ks[10], (DEPTH, D, IN_WIDTH), D ** -0.5),
        "lb_logits": nrm(ks[11], (DEPTH + 1, HGRN_KEY_WIDTH), 0.3),
        "hgrn_norm_g": 1.0 + nrm(ks[12], (DEPTH, HGRN_HEADS, HGRN_DV), 0.02),
        "conv_w": nrm(ks[13], (DEPTH, CONV_K, CONV_WIDTH), CONV_K ** -0.5),
        "conv_b": nrm(ks[14], (DEPTH, CONV_WIDTH), 0.02),
        "w_out_hgrn": nrm(ks[15], (DEPTH, HGRN_VAL_WIDTH, D), HGRN_VAL_WIDTH ** -0.5),
        "w_out_conv": nrm(ks[16], (DEPTH, CONV_WIDTH, D), CONV_WIDTH ** -0.5),
        "w_o": nrm(ks[17], (DEPTH, D, D), D ** -0.5),
        "w_router": nrm(ks[18], (DEPTH, D, N_EXPERTS), D ** -0.5),
        "router_bias": nrm(ks[19], (DEPTH, N_EXPERTS), 0.01),
        "w_exp_gate": nrm(ks[20], (DEPTH, N_EXPERTS, D, EXPERT_FF), D ** -0.5),
        "w_exp_up": nrm(ks[21], (DEPTH, N_EXPERTS, D, EXPERT_FF), D ** -0.5),
        "w_exp_down": nrm(ks[22], (DEPTH, N_EXPERTS, EXPERT_FF, D), EXPERT_FF ** -0.5),
        "w_sh_gate": nrm(ks[23], (DEPTH, D, SHARED_FF), D ** -0.5),
        "w_sh_up": nrm(ks[24], (DEPTH, D, SHARED_FF), D ** -0.5),
        "w_sh_down": nrm(ks[25], (DEPTH, SHARED_FF, D), SHARED_FF ** -0.5),
        "final_norm_g": 1.0 + nrm(ks[26], (D,), 0.02),
    }

def reference(x_prompt, x_sample, state_hgrn, state_conv, c_prompt, c_sample,
              w_ada, b_ada, norm_mix_g, norm_ffn_g, w_in, lb_logits, hgrn_norm_g,
              conv_w, conv_b, w_out_hgrn, w_out_conv, w_o, w_router, router_bias,
              w_exp_gate, w_exp_up, w_exp_down, w_sh_gate, w_sh_up, w_sh_down, final_norm_g):
    lb_all = jnp.cumsum(jax.nn.softmax(lb_logits.astype(jnp.float32), axis=0), axis=0)
    bp = x_prompt.shape[0]
    xp, xs = x_prompt, x_sample
    zero_h = jnp.zeros((bp, HGRN_HEADS, HGRN_DK, HGRN_DV), x_prompt.dtype)
    zero_c = jnp.zeros((bp, CONV_K - 1, CONV_WIDTH), x_prompt.dtype)
    hp_list, cp_list, hs_list, cs_list = [], [], [], []
    for l in range(DEPTH):
        p = {
            "w_ada": w_ada[l], "b_ada": b_ada[l], "norm_mix_g": norm_mix_g[l], "norm_ffn_g": norm_ffn_g[l],
            "w_in": w_in[l], "hgrn_norm_g": hgrn_norm_g[l], "conv_w": conv_w[l], "conv_b": conv_b[l],
            "w_out_hgrn": w_out_hgrn[l], "w_out_conv": w_out_conv[l], "w_o": w_o[l],
            "w_router": w_router[l], "router_bias": router_bias[l],
            "w_exp_gate": w_exp_gate[l], "w_exp_up": w_exp_up[l], "w_exp_down": w_exp_down[l],
            "w_sh_gate": w_sh_gate[l], "w_sh_up": w_sh_up[l], "w_sh_down": w_sh_down[l],
        }
        xp, hp, cp = layer(xp, c_prompt, zero_h, zero_c, lb_all[l], p)
        xs, hs, cs = layer(xs, c_sample, state_hgrn[l], state_conv[l], lb_all[l], p)
        hp_list.append(hp)
        cp_list.append(cp)
        hs_list.append(hs)
        cs_list.append(cs)
    y_prompt = rmsnorm(xp, final_norm_g)
    y_sample = rmsnorm(xs, final_norm_g)
    return (y_prompt, y_sample, jnp.stack(hp_list), jnp.stack(cp_list), jnp.stack(hs_list), jnp.stack(cs_list))


_drawn_inputs = setup_inputs


def setup_inputs(seed=0):
    import zlib

    import numpy as np

    out = dict(_drawn_inputs(seed))
    spreads = {}
    factors = {'hgrn_norm_g': 6.661, 'conv_b': 5.257, 'final_norm_g': 2.766}
    for name, (base, spread) in spreads.items():
        noise = np.random.default_rng([zlib.crc32(name.encode()), seed]).standard_normal(out[name].shape)
        drawn = base * np.exp(spread * noise) if base else spread * noise
        out[name] = __import__('jax').numpy.asarray(drawn.astype(out[name].dtype))
    for name, factor in factors.items():
        out[name] = (out[name] * factor).astype(out[name].dtype)
    return out
```

```python
from contextlib import ExitStack

import numpy as np

import concourse.bass as bass
from concourse import mybir

ALU = mybir.AluOpType
ACT = mybir.ActivationFunctionType
AX = mybir.AxisListType
F32 = mybir.dt.float32
BF16 = mybir.dt.bfloat16
I32 = mybir.dt.int32
U32 = mybir.dt.uint32

P = 128
D = 1024
KD = D // P
T = 1024
NS = 8
TT = T + NS
TILES = T // P + 1
PIECE = TT // 3
PIECES = TT // PIECE
H = 4
HK = 128
W = 512
CH = W // P
CHUNK = 32
CPG = P // CHUNK
GROUPS = T // P
E = 64
EG = 8
FF = 256
TOPK, TOPG = 8, 4
SCALE = 2.5
EPS = 1e-6
ROW0 = 1
ROWS = ROW0 + TT + P
XW = D + E
ITEMS = 2 * E
SPAN = 8
AHEAD = 4
LISTS = 8
RING = 4
NEG = -1e30


def rows_of(t):
    return P if t < TILES - 1 else NS


class Steps:

    def __init__(self, eng, sem):
        self.eng, self.sem, self.n, self.shift = eng, sem, 0, 0

    def run(self, ins):
        ins.then_inc(self.sem, 1)
        self.n += 1

    def settle(self):
        self.eng.wait_ge(self.sem, self.shift + self.n)

    def link(self, ins):
        self.run(ins)
        self.settle()

    def enter(self, i, per):
        self.at, self.per = self.n, per
        self.shift = i * per

    def leave(self, times):
        assert self.n - self.at == self.per, (self.n - self.at, self.per)
        self.shift = 0
        self.n = self.at + self.per * times


def layer(nc, a, o):
    with ExitStack() as top:
        stage = top.enter_context(ExitStack())
        held = []

        def sem(name):
            held.append(stage.enter_context(nc.semaphore(name)))
            return held[-1]

        def next_stage():
            with nc.Block() as block:
                @block.gpsimd
                def _(pool):
                    for s in held:
                        pool.sem_clear(s)
            held.clear()
            stage.close()

        def sb(name, shape, dt=F32, ctx=top):
            return ctx.enter_context(nc.sbuf_tensor(name, shape, dt))

        banks = [top.enter_context(nc.psum_tensor(f"bank{i}", [P, 512], F32)) for i in range(8)]

        mod_d = nc.dram_tensor("mod_d", [NS + 1, 6 * D], F32).ap()
        x2_d = nc.dram_tensor("x2_d", [TT, D], F32).ap()
        xe_d = nc.dram_tensor("xe_d", [ROWS, XW], F32).ap()
        acc_d = nc.dram_tensor("acc_d", [ROWS, D], F32).ap()

        ident = sb("ident", [P, P])
        eps = sb("eps", [P, 1])
        hT = sb("hT", [P, KD, TT])

        x_p = a["x_prompt"].rearrange("b t d -> (b t) d")
        x_s = a["x_sample"].rearrange("b t d -> (b t) d")

        def x_rows(t):
            return x_p[t * P:(t + 1) * P, :] if t < TILES - 1 else x_s

        w_in = a["w_in"].rearrange("l (k p) n -> p (l k) n", p=P)

        NPAR = KD + 2 * CH + H + 3 * CH + CH
        par = sb("par", [P, NPAR])
        with ExitStack() as c1:
            par_rows = sb("par_rows", [NPAR, P], ctx=c1)
            c_rows = sb("c_rows", [NS + 1, D], ctx=c1)
            cT = sb("cT", [P, KD, NS + 1], ctx=c1)
            wada = sb("wada", [P, 3, KD, 512], ctx=c1)
            bada = sb("bada", [NS + 1, 6 * D], ctx=c1)
            mod = sb("mod", [NS + 1, 6 * D], ctx=c1)
            modT = sb("modT", [P, 2 * KD, NS + 1], ctx=c1)
            xn = sb("xn", [P, TILES, D], ctx=c1)
            junk = sb("junk", [P, D], ctx=c1)
            ssq = sb("ssq", [P, TILES], ctx=c1)
            rstd = sb("rstd", [P, TILES], ctx=c1)
            par_in, c_in, b_in, x_in = sem("par_in"), sem("c_in"), sem("b_in"), sem("x_in")
            ada_in = [sem(f"ada_in{i}") for i in range(3)]
            ident_ok, par_T, par_ok, c_ok, cT_ok, cT_cp = (
                sem(n) for n in ("ident_ok", "par_T", "par_ok", "c_ok", "cT_ok", "cT_cp"))
            mod_ps, mod_ok, modT_ps, modT_ok, mod_out = (
                sem(n) for n in ("mod_ps", "mod_ok", "modT_ps", "modT_ok", "mod_out"))
            ssq_ok, sd_ok, xn_ok, xT_ps, hT_ok, hT_s_ok = (
                sem(n) for n in ("ssq_ok", "sd_ok", "xn_ok", "xT_ps", "hT_ok", "hT_s_ok"))
            dve1, pool1, act1 = sem("dve1"), sem("pool1"), sem("act1")
            NADA = 6 * D // 512
            ada_v = a["w_ada"].rearrange("l (k p) n -> p (l k) n", p=P)
            O_G, O_LB, O_HG, O_CW, O_CB = 0, KD, KD + 2 * CH, KD + 2 * CH + H, KD + 2 * CH + H + 3 * CH
            with nc.Block() as block:
                @block.sync
                def _(sp):
                    for at, src in ((O_G, a["norm_mix_g"].rearrange("l (k p) -> (l k) p", p=P)),
                                    (O_LB, a["lb_logits"].rearrange("l (k p) -> (l k) p", p=P)),
                                    (O_HG, a["hgrn_norm_g"].rearrange("l h p -> (l h) p")),
                                    (O_CW, a["conv_w"].rearrange("l j (k p) -> (l j k) p", p=P)),
                                    (O_CB, a["conv_b"].rearrange("l (k p) -> (l k) p", p=P))):
                        sp.dma_start(par_rows[at:at + src.shape[0], :], src).then_inc(par_in, 16)
                    sp.dma_start(c_rows[0:NS, :], a["c_sample"]).then_inc(c_in, 16)
                    sp.dma_start(c_rows[NS:NS + 1, :], a["c_prompt"]).then_inc(c_in, 16)
                    sp.dma_start(bada[:], a["b_ada"].to_broadcast([NS + 1, 6 * D])).then_inc(b_in, 16)
                    for n in range(NADA):
                        if n >= 3:
                            sp.wait_ge(mod_ps, n - 2)
                        sp.dma_start(wada[:, n % 3], ada_v[:, :, n * 512:(n + 1) * 512]).then_inc(ada_in[n % 3], 16)
                    sp.wait_ge(mod_ok, NADA)
                    sp.dma_start(mod_d, mod[:]).then_inc(mod_out, 16)
                    sp.wait_ge(mod_out, 16)

                @block.gpsimd
                def _(pool):
                    pool.memset(ident[:], 0.0).then_inc(pool1, 1)
                    pool.wait_ge(pool1, 1)
                    pool.affine_select(out=ident[:], in_=ident[:], compare_op=ALU.not_equal, fill=1.0, base=0,
                                       pattern=[[-1, P]], channel_multiplier=1).then_inc(ident_ok, 1)
                    pool.memset(eps[:], EPS).then_inc(ident_ok, 1)

                @block.scalar
                def _(act):
                    for t in range(TILES):
                        act.dma_start(xn[0:rows_of(t), t, :], x_rows(t)).then_inc(x_in, 16)
                    act.wait_ge(c_in, 32)
                    act.activation(c_rows[:], c_rows[:], ACT.Silu).then_inc(c_ok, 1)
                    act.wait_ge(x_in, 16 * TILES)
                    for t in range(TILES):
                        if t:
                            act.wait_ge(ssq_ok, t)
                        act.activation(junk[0:rows_of(t), :], xn[0:rows_of(t), t, :], ACT.Square,
                                       accum_out=ssq[0:rows_of(t), t:t + 1]).then_inc(ssq_ok, 1)
                    act.wait_ge(ident_ok, 2)
                    act.wait_ge(ssq_ok, TILES)
                    act.activation(rstd[:, 0:TILES - 1], ssq[:, 0:TILES - 1], ACT.Sqrt, scale=1.0 / D,
                                   bias=eps[:, 0:1]).then_inc(sd_ok, 1)
                    act.activation(rstd[0:NS, TILES - 1:], ssq[0:NS, TILES - 1:], ACT.Sqrt, scale=1.0 / D,
                                   bias=eps[0:NS, 0:1]).then_inc(sd_ok, 1)
                    act.wait_ge(modT_ok, 1)
                    for k in range(KD):
                        act.wait_ge(xT_ps, 2 * k + 1)
                        act.activation(hT[:, k, 0:512], banks[2 + (2 * k) % 4][:], ACT.Identity,
                                       scale=modT[:, KD + k, NS:NS + 1], bias=modT[:, k, NS:NS + 1]).then_inc(hT_ok, 1)

                @block.tensor
                def _(pe):
                    pe.wait_ge(ident_ok, 1)
                    pe.wait_ge(par_in, 16 * 5)
                    pe.transpose(banks[0][:, 0:NPAR], par_rows[:], ident[0:NPAR, 0:NPAR]).then_inc(par_T, 1)
                    pe.wait_ge(c_ok, 1)
                    for k in range(KD):
                        last = pe.transpose(banks[1][:, k * (NS + 1):(k + 1) * (NS + 1)], c_rows[:, k * P:(k + 1) * P],
                                            ident[0:NS + 1, 0:NS + 1])
                    last.then_inc(cT_ok, 1)
                    pe.wait_ge(cT_cp, 1)

                    def cond(n):
                        pe.wait_ge(ada_in[n % 3], 16 * (n // 3 + 1))
                        if n >= 2:
                            pe.wait_ge(mod_ok, n - 1)
                        for k in range(KD):
                            last = pe.matmul(banks[n % 2][0:NS + 1, :], cT[:, k, :], wada[:, n % 3, k, :],
                                             start=(k == 0), stop=(k == KD - 1))
                        last.then_inc(mod_ps, 1)

                    for n in range(4):
                        cond(n)
                    pe.wait_ge(mod_ok, 4)
                    for k in range(2 * KD):
                        last = pe.transpose(banks[2][:, k * (NS + 1):(k + 1) * (NS + 1)], mod[:, k * P:(k + 1) * P],
                                            ident[0:NS + 1, 0:NS + 1])
                    last.then_inc(modT_ps, 1)
                    pe.wait_ge(modT_ok, 1)
                    pe.wait_ge(xn_ok, TILES)
                    for k in range(KD):
                        for half in range(2):
                            n = 2 * k + half
                            if n >= 4:
                                pe.wait_ge((hT_ok, hT_s_ok)[half], k - 1)
                            for j in range(4):
                                t = 4 * half + j
                                last = pe.transpose(banks[2 + n % 4][:, j * P:(j + 1) * P], xn[:, t, k * P:(k + 1) * P],
                                                    ident[:])
                            last.then_inc(xT_ps, 1)
                    for k in range(KD):
                        last = pe.transpose(banks[6][:, k * NS:(k + 1) * NS], xn[0:NS, TILES - 1, k * P:(k + 1) * P],
                                            ident[0:NS, 0:NS])
                    last.then_inc(xT_ps, 1)
                    for n in range(4, NADA):
                        cond(n)

                @block.vector
                def _(dve):
                    s = Steps(dve, dve1)
                    dve.wait_ge(par_T, 1)
                    s.link(dve.tensor_copy(par[:], banks[0][:, 0:NPAR]))
                    dve.wait_ge(cT_ok, 1)
                    dve.tensor_copy(cT[:].rearrange("p k c -> p (k c)"), banks[1][:, 0:KD * (NS + 1)]).then_inc(cT_cp, 1)
                    dve.wait_ge(sd_ok, 2)
                    s.run(dve.reciprocal(rstd[:, 0:TILES - 1], rstd[:, 0:TILES - 1]))
                    s.link(dve.reciprocal(rstd[0:NS, TILES - 1:], rstd[0:NS, TILES - 1:]))
                    for t in range(TILES):
                        r = rows_of(t)
                        dve.tensor_scalar(xn[0:r, t, :], xn[0:r, t, :], rstd[0:r, t:t + 1], None,
                                          ALU.mult).then_inc(xn_ok, 1)

                    def cond(n):
                        dve.wait_ge(mod_ps, n + 1)
                        dve.tensor_tensor(mod[:, n * 512:(n + 1) * 512], banks[n % 2][0:NS + 1, :],
                                          bada[:, n * 512:(n + 1) * 512], ALU.add).then_inc(mod_ok, 1)

                    dve.wait_ge(b_in, 16)
                    for n in range(4):
                        cond(n)
                    dve.wait_ge(modT_ps, 1)
                    s.run(dve.tensor_copy(modT[:, 0:KD].rearrange("p k c -> p (k c)"), banks[2][:, 0:KD * (NS + 1)]))
                    m = KD * (NS + 1)
                    s.link(dve.tensor_scalar(modT[:, KD:].rearrange("p k c -> p (k c)"), banks[2][:, m:2 * m], 1.0, None,
                                             ALU.add))
                    dve.tensor_tensor(modT[:, KD:], modT[:, KD:],
                                      par[:, O_G:O_G + KD].unsqueeze(2).to_broadcast([P, KD, NS + 1]),
                                      ALU.mult).then_inc(modT_ok, 1)
                    dve.wait_ge(modT_ok, 1)
                    for k in range(KD):
                        dve.wait_ge(xT_ps, 2 * k + 2)
                        dve.tensor_scalar(hT[:, k, 512:T], banks[2 + (2 * k + 1) % 4][:], modT[:, KD + k, NS:NS + 1],
                                          modT[:, k, NS:NS + 1], ALU.mult, ALU.add).then_inc(hT_s_ok, 1)
                    dve.wait_ge(xT_ps, 2 * KD + 1)
                    s.link(dve.tensor_tensor(hT[:, :, T:], banks[6][:, 0:KD * NS].rearrange("p (k c) -> p k c", c=NS),
                                             modT[:, KD:, 0:NS], ALU.mult))
                    s.link(dve.tensor_tensor(hT[:, :, T:], hT[:, :, T:], modT[:, 0:KD, 0:NS], ALU.add))
                    for n in range(4, NADA):
                        cond(n)

        with ExitStack() as c2:
            qT = sb("qT", [P, CH, TT], ctx=c2)
            gT = sb("gT", [P, CH, TT], ctx=c2)
            bT = sb("bT", [P, CH, TT], ctx=c2)
            with ExitStack() as c3:
                fT = sb("fT", [P, CH, TT], ctx=c3)
                cvT = sb("cvT", [P, CH, TT], ctx=c3)
                vv = sb("vv", [P, TILES, W], ctx=c3)
                with ExitStack() as c4:
                    next_stage()
                    project_in(nc, a, c4, sb, sem, banks, w_in, hT, qT, fT, gT, bT, cvT, vv)
                next_stage()
                token_mixers(nc, a, o, sb, sem, banks, par, ident, eps, qT, fT, gT, bT, cvT, vv,
                             (O_LB, O_HG, O_CW, O_CB))
            mT = sb("mT", [P, KD, TT], ctx=c2)
            next_stage()
            merge(nc, a, sb, sem, banks, w_in, hT, qT, bT, mT)
            next_stage()
            output_and_norm(nc, a, sb, sem, banks, ident, eps, mod_d, x2_d, xe_d, x_rows, mT, hT)
        with ExitStack() as c5:
            wexp = sb("wexp", [P, RING, KD + 4, 512], ctx=c5)
            posm = sb("posm", [P, E + 1, TILES], ctx=c5)
            table = sb("table", [1, ITEMS + AHEAD, 2], I32, ctx=c5)
            total = sb("total", [1, 1], I32, ctx=c5)
            tok = sb("tok", [P, TILES, 2], BF16, ctx=c5)
            idle = sb("idle", [P, 1], ctx=c5)
            iota = sb("iota", [P, TILES * P], ctx=c5)
            next_stage()
            slot_in = [top.enter_context(nc.semaphore(f"slot_in{i}")) for i in range(RING)]
            routing(nc, a, sb, sem, banks, hT, xe_d, acc_d, posm, table, total, tok, idle, iota, wexp, slot_in)
            next_stage()
            experts(nc, a, sb, sem, banks, ident, xe_d, acc_d, posm, table, total, tok, idle, iota, wexp, slot_in)
        next_stage()
        final(nc, a, o, sb, sem, eps, mod_d, x2_d, acc_d)


def project_in(nc, a, ctx, sb, sem, banks, w_in, hT, qT, fT, gT, bT, cvT, vv):
    U = 2 * P
    wA = sb("wA", [P, KD, U], ctx=ctx)
    wB = sb("wB", [P, KD, U], ctx=ctx)
    tmp = sb("vtmp", [P, 2, PIECE], ctx=ctx)
    w_ready = [sem("winA"), sem("winB")]
    w_used = sem("win_used")
    ps_full, ps_read = sem("proj_full"), sem("proj_read")
    tmp_ok, tmp_used = sem("vtmp_ok"), sem("vtmp_used")
    bufs = (wA, wB)
    PER = 2 * CH // 2 * PIECES
    VPER = 2 * TILES
    NB = 6
    units = 7 * 2
    with nc.Block() as block:
        @block.sync
        def _(sp):
            for j in range(2):
                sp.dma_start(bufs[j][:], w_in[:, :, j * U:(j + 1) * U]).then_inc(w_ready[j], 16)
            with sp.Fori(1, units // 2) as i:
                for j in range(2):
                    sp.wait_ge(w_used, 2 * i - 1 + j)
                    sp.dma_start(bufs[j][:], w_in[:, :, bass.ds(i * (2 * U) + j * U, U)]).then_inc(w_ready[j], 16)

        @block.tensor
        def _(pe):
            def tensor_pass(i, first):
                for j in range(2):
                    pe.wait_ge(w_ready[j], 16 * i + 16)
                    for c in range(2):
                        for n in range(PIECES):
                            r = (2 * j + c) * PIECES + n
                            pe.wait_ge(ps_read, first + r + 1)
                            for k in range(KD):
                                last = pe.matmul(banks[r % NB][:, 0:PIECE], bufs[j][:, k, c * P:(c + 1) * P],
                                                 hT[:, k, n * PIECE:(n + 1) * PIECE], start=(k == 0), stop=(k == KD - 1))
                            last.then_inc(ps_full, 1)
                    pe.matmul(banks[7][:, 0:1], bufs[j][:, 0, 0:P], bufs[j][:, 0, 0:1], start=True, stop=True).then_inc(w_used, 1)

            with pe.Fori(0, 2) as i:
                tensor_pass(i, i * PER)
            for j in range(2):
                pe.wait_ge(w_ready[j], 16 * 3)
                for t in range(TILES):
                    r = j * TILES + t
                    pe.wait_ge(ps_read, 2 * PER + r + 1)
                    m = rows_of(t)
                    for k in range(KD):
                        last = pe.matmul(banks[r % NB][0:m, 0:U], hT[:, k, t * P:t * P + m], bufs[j][:, k, :],
                                         start=(k == 0), stop=(k == KD - 1))
                    last.then_inc(ps_full, 1)
                pe.matmul(banks[7][:, 0:1], bufs[j][:, 0, 0:P], bufs[j][:, 0, 0:1], start=True, stop=True).then_inc(w_used, 1)
            with pe.Fori(3, 7) as i:
                tensor_pass(i, (i - 1) * PER + VPER)

        @block.scalar
        def _(act):
            act.sem_inc(ps_read, NB)

            def take(dst, func, first):
                for c in range(CH):
                    for n in range(PIECES):
                        r = c * PIECES + n
                        act.wait_ge(ps_full, first + r + 1)
                        act.activation(dst[:, c, n * PIECE:(n + 1) * PIECE], banks[r % NB][:, 0:PIECE],
                                       func).then_inc(ps_read, 1)

            take(qT, ACT.Silu, 0)
            take(fT, ACT.Sigmoid, PER)
            for r in range(VPER):
                act.wait_ge(ps_full, 2 * PER + r + 1)
                j, t = divmod(r, TILES)
                m = rows_of(t)
                act.activation(vv[0:m, t, j * U:(j + 1) * U], banks[r % NB][0:m, 0:U], ACT.Copy).then_inc(ps_read, 1)
            take(gT, ACT.Silu, 2 * PER + VPER)
            take(bT, ACT.Copy, 3 * PER + VPER)
            take(cvT, ACT.Copy, 4 * PER + VPER)
            for c in range(CH):
                for n in range(PIECES):
                    r = c * PIECES + n
                    act.wait_ge(ps_full, 5 * PER + VPER + r + 1)
                    if r >= 2:
                        act.wait_ge(tmp_used, r - 1)
                    act.activation(tmp[:, r % 2, :], banks[r % NB][:, 0:PIECE], ACT.Copy).then_inc(tmp_ok, 1)
                    act.wait_ge(tmp_ok, r + 1)
                    act.sem_inc(ps_read, 1)

        @block.vector
        def _(dve):
            for r in range(PER):
                c, n = divmod(r, PIECES)
                dve.wait_ge(tmp_ok, r + 1)
                at = cvT[:, c, n * PIECE:(n + 1) * PIECE]
                dve.tensor_tensor(at, at, tmp[:, r % 2, :], ALU.mult).then_inc(tmp_used, 1)


def token_mixers(nc, a, o, sb, sem, banks, par, ident, eps, qT, fT, gT, bT, cvT, vv, offsets):
    O_LB, O_HG, O_CW, O_CB = offsets
    with ExitStack() as ctx:
        def tile(name, shape, dt=F32):
            return sb(name, shape, dt, ctx)

        onesm = tile("onesm", [P, P])
        chunks = ExitStack()
        tile = lambda name, shape, dt=F32: sb(name, shape, dt, chunks)
        lb = tile("lb", [P, H])
        omlb = tile("omlb", [P, H])
        lbt = tile("lbt", [P, 4, H])
        reset = tile("reset", [P, W])
        causal = tile("causal", [P, H, P], I32)
        lnf = tile("lnf", [P, 2, W])
        cum = tile("cum", [P, 2, W])
        ex = tile("ex", [P, 2, W])
        exi = tile("exi", [P, 2, W])
        exe = tile("exe", [P, 2, W])
        rest = lnf
        kk = tile("kk", [P, W])
        qin = tile("qin", [P, 2, W])
        kin = tile("kin", [P, 2, W])
        kend = tile("kend", [P, 2, W])
        kendR = tile("kendR", [P, W])
        vst = tile("vst", [P, 2, W])
        attm = tile("attm", [P, 2, W])
        S = tile("S", [P, CPG + 1, W])

        names = ("mk_lb mk_ln mk_cum mk_exp mk_rest mk_exe mk_q mk_k mk_kT mk_kR mk_att mk_am mk_v mk_U mk_S "
                 "mk_o mk_oc mk_f mk_const").split()
        (lb_ok, ln_ok, cum_ok, exp_ok, rest_ok, exe_ok, qk_ok, kend_ok, kT_ps, kR_ok, att_ps, am_ok, v_ok,
         U_ps, S_ok, o_ps, o_ok, f_ok, const_ok) = (sem(n) for n in names)
        dve2, pool2 = sem("dve2"), sem("pool2")
        st_out = sem("st_out")
        passed = sem("mk_passed")
        att_b, kT_b, o_b = banks[4], banks[5], banks[6]

        def grp(x, g):
            return x[:, :, bass.ds(g * P, P)]

        def h3(x):
            return x.rearrange("p (h t) -> p h t", h=H)

        def slot(b, j):
            return (CPG * b + j) % (2 * CPG) if j in (0, CPG) else j

        with nc.Block() as block:
            @block.gpsimd
            def _(pool):
                pool.memset(reset[:], 1.0).then_inc(pool2, 1)
                pool.memset(onesm[:], 1.0).then_inc(const_ok, 1)
                pool.memset(causal[:], 1).then_inc(pool2, 1)
                pool.wait_ge(pool2, 2)
                pool.memset(reset[:].rearrange("p (c t) -> p c t", t=CHUNK)[:, :, 0:1], 0.0).then_inc(const_ok, 1)
                pool.affine_select(out=causal[:], in_=causal[:], compare_op=ALU.is_ge, fill=0.0, base=0,
                                   pattern=[[0, H], [1, P]], channel_multiplier=-1).then_inc(pool2, 1)
                for c in range(1, CPG):
                    pool.wait_ge(pool2, 2 + c)
                    v = causal[:, :, c * CHUNK:(c + 1) * CHUNK]
                    pool.affine_select(out=v, in_=v, compare_op=ALU.is_ge, fill=0.0, base=-c * CHUNK,
                                       pattern=[[0, H], [0, CHUNK]], channel_multiplier=1).then_inc(pool2, 1)
                pool.wait_ge(pool2, 2 + CPG)
                pool.memset(attm[:], 0.0).then_inc(const_ok, 1)
                pool.memset(S[:, 0, :], 0.0).then_inc(const_ok, 1)

            @block.scalar
            def _(act):
                act.wait_ge(lb_ok, 1)
                act.activation(lbt[:, 0:2, :], lbt[:, 0:2, :], ACT.Exp).then_inc(lb_ok, 1)
                act.wait_ge(f_ok, 1)
                with act.Fori(0, GROUPS // 2) as i:
                    for b in range(2):
                        g = 2 * i + b
                        act.activation(h3(lnf[:, b]), grp(fT, g), ACT.Ln).then_inc(ln_ok, 1)
                        act.activation(vst[:, b], vv[:, bass.ds(g, 1), :].rearrange("p a n -> p (a n)"),
                                       ACT.Copy).then_inc(v_ok, 1)
                        act.wait_ge(cum_ok, g + 1)
                        act.activation(ex[:, b], cum[:, b], ACT.Exp).then_inc(exp_ok, 1)
                        act.activation(exi[:, b], cum[:, b], ACT.Exp, scale=-1.0).then_inc(exp_ok, 1)
                        act.wait_ge(rest_ok, g + 1)
                        act.activation(exe[:, b], rest[:, b], ACT.Exp).then_inc(exe_ok, 1)
                        act.wait_ge(kT_ps, g + 1)
                        act.activation(kendR[:], kT_b[:], ACT.Copy).then_inc(kR_ok, 1)
                        act.wait_ge(o_ps, g + 1)
                        act.activation(grp(qT, g), h3(o_b[:]), ACT.Copy).then_inc(o_ok, 1)

            @block.vector
            def _(dve):
                s = Steps(dve, dve2)
                l0, l1 = par[:, O_LB:O_LB + H], par[:, O_LB + H:O_LB + 2 * H]
                s.link(dve.tensor_tensor(lbt[:, 2, :], l0, l1, ALU.max))
                s.run(dve.tensor_tensor(lbt[:, 0, :], l0, lbt[:, 2, :], ALU.subtract))
                s.run(dve.tensor_tensor(lbt[:, 1, :], l1, lbt[:, 2, :], ALU.subtract))
                s.settle()
                dve.sem_inc(lb_ok, 1)
                dve.wait_ge(lb_ok, 2)
                s.link(dve.tensor_tensor(lbt[:, 2, :], lbt[:, 0, :], lbt[:, 1, :], ALU.add))
                s.link(dve.reciprocal(lbt[:, 3, :], lbt[:, 2, :]))
                s.link(dve.tensor_tensor(lb[:], lbt[:, 0, :], lbt[:, 3, :], ALU.mult))
                s.link(dve.tensor_scalar(omlb[:], lb[:], -1.0, 1.0, ALU.mult, ALU.add))
                for h in range(H):
                    s.run(dve.tensor_scalar(fT[:, h, :], fT[:, h, :], omlb[:, h:h + 1], lb[:, h:h + 1], ALU.mult, ALU.add))
                s.settle()
                dve.sem_inc(f_ok, 1)
                dve.wait_ge(const_ok, 4)
                with dve.Fori(0, GROUPS // 2) as i:
                    PER = 2 * (3 + CPG * H)
                    s.enter(i, PER)
                    for b in range(2):
                        g = 2 * i + b
                        dve.wait_ge(ln_ok, g + 1)
                        dve.tensor_tensor_scan(cum[:, b], reset[:], lnf[:, b], 0.0, ALU.mult, ALU.add).then_inc(cum_ok, 1)
                        s.run(dve.tensor_scalar(h3(kk[:]), grp(fT, g), -1.0, 1.0, ALU.mult, ALU.add))
                        dve.wait_ge(cum_ok, g + 1)
                        c3 = cum[:, b].rearrange("p (c t) -> p c t", t=CHUNK)
                        dve.tensor_tensor(rest[:, b].rearrange("p (c t) -> p c t", t=CHUNK),
                                          c3[:, :, CHUNK - 1:CHUNK].to_broadcast([P, H * CPG, CHUNK]), c3,
                                          ALU.subtract).then_inc(rest_ok, 1)
                        dve.wait_ge(exp_ok, 2 * g + 2)
                        s.settle()
                        s.run(dve.tensor_tensor(h3(qin[:, b]), grp(qT, g), h3(ex[:, b]), ALU.mult))
                        s.run(dve.tensor_tensor(kin[:, b], kk[:], exi[:, b], ALU.mult))
                        s.settle()
                        dve.sem_inc(qk_ok, 1)
                        dve.wait_ge(exe_ok, g + 1)
                        dve.tensor_tensor(kend[:, b], kk[:], exe[:, b], ALU.mult).then_inc(kend_ok, 1)
                        dve.wait_ge(att_ps, g + 1)
                        dve.sem_inc(passed, 1)
                        dve.copy_predicated(attm[:, b], causal[:].rearrange("p h t -> p (h t)"),
                                            att_b[:]).then_inc(am_ok, 1)
                        dve.wait_ge(U_ps, g + 1)
                        for j in range(CPG):
                            for h in range(H):
                                at = slice(h * HK, (h + 1) * HK)
                                last = h * P + j * CHUNK + CHUNK - 1
                                s.run(dve.scalar_tensor_tensor(
                                    out=S[:, slot(b, j + 1), at], in0=S[:, slot(b, j), at],
                                    scalar=ex[:, b, last:last + 1], in1=banks[j][:, at], op0=ALU.mult, op1=ALU.add))
                            s.settle()
                            if j == CPG - 2:
                                dve.sem_inc(S_ok, 1)
                            if j == CPG - 1:
                                dve.sem_inc(S_ok, 1)
                    s.leave(GROUPS // 2)

            @block.tensor
            def _(pe):
                for ahead in (am_ok, kR_ok, S_ok, o_ok):
                    pe.sem_inc(ahead, 1)
                with pe.Fori(0, GROUPS // 2) as i:
                    for b in range(2):
                        g = 2 * i + b
                        pe.wait_ge(qk_ok, g + 1)
                        pe.wait_ge(am_ok, g + 1)
                        for h in range(H):
                            at = slice(h * HK, (h + 1) * HK)
                            last = pe.matmul(att_b[:, at], kin[:, b, at], qin[:, b, at], start=True, stop=True)
                        last.then_inc(att_ps, 1)
                        pe.wait_ge(kend_ok, g + 1)
                        pe.wait_ge(kR_ok, g + 1)
                        for h in range(H):
                            at = slice(h * HK, (h + 1) * HK)
                            last = pe.transpose(kT_b[:, at], kend[:, b, at], ident[:])
                        last.then_inc(kT_ps, 1)
                        pe.wait_ge(kR_ok, g + 2)
                        pe.wait_ge(v_ok, g + 1)
                        pe.wait_ge(S_ok, 2 * g + 1)
                        for j in range(CPG):
                            rows = slice(j * CHUNK, (j + 1) * CHUNK)
                            for h in range(H):
                                at = slice(h * HK, (h + 1) * HK)
                                last = pe.matmul(banks[j][:, at], kendR[rows, at], vst[rows, b, at],
                                                 start=True, stop=True)
                        last.then_inc(U_ps, 1)
                        pe.wait_ge(am_ok, g + 2)
                        pe.wait_ge(S_ok, 2 * g + 2)
                        pe.wait_ge(o_ok, g + 1)
                        for h in range(H):
                            at = slice(h * HK, (h + 1) * HK)
                            pe.matmul(o_b[:, at], vst[:, b, at], attm[:, b, at], start=(h == 0), stop=False,
                                      skip_group_check=True)
                        for h in range(H):
                            for j in range(CPG):
                                cols = slice(h * P + j * CHUNK, h * P + (j + 1) * CHUNK)
                                last = pe.matmul(o_b[:, cols], S[:, slot(b, j), h * HK:(h + 1) * HK], qin[:, b, cols],
                                                 start=False, stop=(h == H - 1 and j == CPG - 1), skip_group_check=True)
                        last.then_inc(o_ps, 1)

            @block.sync
            def _(sp):
                sp.wait_ge(S_ok, 2 * GROUPS + 1)
                sp.dma_start(o["hgrn_prompt"].rearrange("l b h d v -> d (l b h) v"),
                             S[:, 0, :].rearrange("p (h v) -> p h v", h=H)).then_inc(st_out, 16)
                sp.wait_ge(st_out, 16)

        chunks.close()
        tile = lambda name, shape, dt=F32: sb(name, shape, dt, ctx)
        conv = tile("conv", [P, T])
        sin = tile("sin", [P, 2, W])
        snew = tile("snew", [P, 2, W])
        stmp = tile("stmp", [P, W])
        sel = tile("sel", [NS, NS, P])
        ks = tile("ks", [P, H, NS])
        cst = tile("cst", [NS * 2, W])
        cstT = tile("cstT", [P, CH, NS * 2])
        cso = tile("cso", [NS + 2, W])
        names = "sm_in0 sm_in1 sm_out0 sm_out1 sm_sel sm_sel0 sm_v sm_new sm_k sm_o sm_oc sm_cs sm_cT sm_cTc sm_u sm_uo sm_co".split()
        (in0, in1, out0, out1, sel_ok, sel0, vb_ps, new_ok, ks_ok, os_ps, os_ok, cs_in, cT_ps, cT_ok, u_ps, u_ok,
         co_out) = (sem(n) for n in names)
        dve3, act3 = sem("dve3"), sem("act3")
        sq_ok, ss_ps, sd2_ok, ya_ok = sem("sq_ok"), sem("ss_ps"), sem("sd2_ok"), sem("ya_ok")
        sq = tile("sq", [P, 2, PIECE])
        sd = tile("sd", [P, 2, PIECE])
        state_in = a["state_hgrn"].rearrange("l b h d v -> d (l b) h v")
        state_out = o["hgrn_sample"].rearrange("l b h d v -> d (l b) h v")
        in_s, out_s = (in0, in1), (out0, out1)
        norm_items = [(h, n) for h in range(H) for n in range(PIECES)]
        with nc.Block() as block:
            @block.sync
            def _(sp):
                sp.dma_start(cst[:], a["state_conv"].rearrange("l b j w -> (l b j) w")).then_inc(cs_in, 16)
                sp.dma_start(o["conv_sample"][:, :, 0, :], a["state_conv"][:, :, 1, :]).then_inc(co_out, 16)
                for b in range(NS):
                    if b >= 2:
                        sp.wait_ge(new_ok, b - 1)
                    sp.dma_start(sin[:, b % 2, :].rearrange("p (h v) -> p h v", h=H),
                                 state_in[:, b]).then_inc(in_s[b % 2], 16)
                sp.wait_ge(u_ok, 1)
                sp.dma_start(o["conv_prompt"].rearrange("l b j w -> (l b j) w"), cso[0:2, :]).then_inc(co_out, 16)
                sp.dma_start(o["conv_sample"][0, :, 1, :], cso[2:, :]).then_inc(co_out, 16)
                sp.wait_ge(co_out, 48)

            @block.gpsimd
            def _(pool):
                pool.memset(sel[:], 0.0).then_inc(sel0, 1)
                pool.wait_ge(sel0, 1)
                pool.affine_select(out=sel[:], in_=sel[:], compare_op=ALU.not_equal, fill=1.0, base=0,
                                   pattern=[[-1, NS], [0, P]], channel_multiplier=1).then_inc(sel_ok, 1)
                for b in range(NS):
                    pool.wait_ge(new_ok, b + 1)
                    pool.dma_start(state_out[:, b], snew[:, b % 2, :].rearrange("p (h v) -> p h v", h=H)).then_inc(
                        out_s[b % 2], 16)
                for b in range(2):
                    pool.wait_ge(out_s[b], 16 * NS // 2)

            @block.tensor
            def _(pe):
                pe.wait_ge(sel_ok, 1)

                def value_rows(b):
                    if b >= 2:
                        pe.wait_ge(new_ok, b - 1)
                    pe.matmul(banks[b % 2][:], sel[:, b, :], vv[0:NS, TILES - 1, :], start=True,
                              stop=True).then_inc(vb_ps, 1)

                value_rows(0)
                pe.wait_ge(cs_in, 16)
                for c in range(CH):
                    last = pe.transpose(banks[3][:, c * 2 * NS:(c + 1) * 2 * NS], cst[:, c * P:(c + 1) * P],
                                        ident[0:2 * NS, 0:2 * NS])
                last.then_inc(cT_ps, 1)
                for c in range(CH):
                    last = pe.transpose(banks[4][0:NS + 2, c * P:(c + 1) * P], cvT[:, c, T - 2:TT], ident[:])
                last.then_inc(u_ps, 1)
                for b in range(NS):
                    if b + 1 < NS:
                        value_rows(b + 1)
                    pe.wait_ge(new_ok, b + 1)
                    for h in range(H):
                        last = pe.matmul(banks[2][:, h * NS + b:h * NS + b + 1], snew[:, b % 2, h * HK:(h + 1) * HK],
                                         qT[:, h, T + b:T + b + 1], start=True, stop=True)
                    last.then_inc(os_ps, 1)
                for r, (h, n) in enumerate(norm_items):
                    pe.wait_ge(sq_ok, r + 1)
                    if r >= 2:
                        pe.wait_ge(sd2_ok, r - 1)
                    pe.matmul(banks[5 + r % 2][:, 0:PIECE], onesm[:], sq[:, r % 2, :], start=True, stop=True).then_inc(ss_ps, 1)

            @block.scalar
            def _(act):
                act.wait_ge(cT_ps, 1)
                act.activation(cstT[:].rearrange("p c n -> p (c n)"), banks[3][:, 0:CH * 2 * NS], ACT.Copy).then_inc(cT_ok, 1)
                act.wait_ge(u_ps, 1)
                act.activation(cso[:], banks[4][0:NS + 2, :], ACT.Copy).then_inc(u_ok, 1)
                act.wait_ge(os_ps, NS)
                act.activation(qT[:, :, T:], banks[2][:, 0:H * NS].rearrange("p (h b) -> p h b", h=H), ACT.Copy).then_inc(os_ok, 1)
                act.wait_ge(os_ok, 1)
                for r, (h, n) in enumerate(norm_items):
                    at = slice(n * PIECE, (n + 1) * PIECE)
                    if r >= 2:
                        act.wait_ge(ss_ps, r - 1)
                    act.activation(sq[:, r % 2, :], qT[:, h, at], ACT.Square).then_inc(sq_ok, 1)
                    act.wait_ge(ss_ps, r + 1)
                    if r >= 2:
                        act.wait_ge(ya_ok, r - 1)
                    act.activation(sd[:, r % 2, :], banks[5 + r % 2][:, 0:PIECE], ACT.Sqrt, scale=1.0 / HK,
                                   bias=eps[:, 0:1]).then_inc(sd2_ok, 1)

            @block.vector
            def _(dve):
                s = Steps(dve, dve3)
                s.link(dve.tensor_scalar(ks[:], fT[:, :, T:], -1.0, 1.0, ALU.mult, ALU.add))
                for b in range(NS):
                    dve.wait_ge(in_s[b % 2], 16 * (b // 2 + 1))
                    if b >= 2:
                        dve.wait_ge(out_s[b % 2], 16 * (b // 2))
                        dve.wait_ge(os_ps, b - 1)
                    dve.wait_ge(vb_ps, b + 1)

                    def h3b(x):
                        return x.rearrange("p (h v) -> p h v", h=H)

                    s.run(dve.tensor_tensor(h3b(snew[:, b % 2]), h3b(sin[:, b % 2]),
                                            fT[:, :, T + b:T + b + 1].to_broadcast([P, H, HK]), ALU.mult))
                    s.run(dve.tensor_tensor(h3b(stmp[:]), h3b(banks[b % 2][:]),
                                            ks[:, :, b:b + 1].to_broadcast([P, H, HK]), ALU.mult))
                    s.settle()
                    dve.tensor_tensor(snew[:, b % 2], snew[:, b % 2], stmp[:], ALU.add).then_inc(new_ok, 1)
                    dve.wait_ge(new_ok, b + 1)
                dve.wait_ge(cT_ok, 1)
                for c in range(CH):
                    w0, w1, w2 = (par[:, O_CW + j * CH + c:O_CW + j * CH + c + 1] for j in range(3))
                    bias = par[:, O_CB + c:O_CB + c + 1]
                    u = cvT[:, c, :]
                    s.link(dve.tensor_scalar(conv[:], u[:, 0:T], w2, bias, ALU.mult, ALU.add))
                    s.link(dve.scalar_tensor_tensor(out=conv[:, 1:], in0=u[:, 0:T - 1], scalar=w1, in1=conv[:, 1:],
                                                    op0=ALU.mult, op1=ALU.add))
                    s.link(dve.scalar_tensor_tensor(out=conv[:, 2:], in0=u[:, 0:T - 2], scalar=w0, in1=conv[:, 2:],
                                                    op0=ALU.mult, op1=ALU.add))
                    s.run(dve.tensor_tensor(bT[:, c, 0:T], bT[:, c, 0:T], conv[:], ALU.mult))
                    old = cstT[:, c, :].rearrange("p (b j) -> p b j", j=2)
                    s.link(dve.tensor_scalar(stmp[:, 0:NS], u[:, T:], w2, bias, ALU.mult, ALU.add))
                    s.link(dve.scalar_tensor_tensor(out=stmp[:, 0:NS], in0=old[:, :, 1], scalar=w1, in1=stmp[:, 0:NS],
                                                    op0=ALU.mult, op1=ALU.add))
                    s.link(dve.scalar_tensor_tensor(out=stmp[:, 0:NS], in0=old[:, :, 0], scalar=w0, in1=stmp[:, 0:NS],
                                                    op0=ALU.mult, op1=ALU.add))
                    s.link(dve.tensor_tensor(bT[:, c, T:], bT[:, c, T:], stmp[:, 0:NS], ALU.mult))
                for r, (h, n) in enumerate(norm_items):
                    at = slice(n * PIECE, (n + 1) * PIECE)
                    dve.wait_ge(sd2_ok, r + 1)
                    s.link(dve.reciprocal(sd[:, r % 2, :], sd[:, r % 2, :]))
                    s.link(dve.scalar_tensor_tensor(out=sd[:, r % 2, :], in0=sd[:, r % 2, :],
                                                    scalar=par[:, O_HG + h:O_HG + h + 1], in1=gT[:, h, at],
                                                    op0=ALU.mult, op1=ALU.mult))
                    dve.tensor_tensor(qT[:, h, at], qT[:, h, at], sd[:, r % 2, :], ALU.mult).then_inc(ya_ok, 1)


def merge(nc, a, sb, sem, banks, w_in, hT, yaT, ybT, mT):
    U = 2 * P
    GA = 7 * W
    with ExitStack() as ctx:
        wga = [sb(f"wga{j}", [P, KD, U], ctx=ctx) for j in range(2)]
        wgb = [sb(f"wgb{j}", [P, KD, U], ctx=ctx) for j in range(2)]
        woa = [sb(f"woa{j}", [P, CH, U], ctx=ctx) for j in range(2)]
        wob = [sb(f"wob{j}", [P, CH, U], ctx=ctx) for j in range(2)]
        sa = sb("sa", [P, 2, PIECE], ctx=ctx)
        sbb = sb("sbb", [P, 2, PIECE], ctx=ctx)
        w_ok = [sem("mg_w0"), sem("mg_w1")]
        gates_ps, gates_ok, outs_ps, free, part = (sem(n) for n in ("mg_gp", "mg_go", "mg_op", "mg_free", "mg_part"))
        out_a = a["w_out_hgrn"].rearrange("l (k p) n -> p (l k) n", p=P)
        out_b = a["w_out_conv"].rearrange("l (k p) n -> p (l k) n", p=P)
        UNITS = D // U
        PER = 2 * PIECES
        with nc.Block() as block:
            @block.sync
            def _(sp):
                def load(at, j):
                    sp.dma_start(wga[j][:], w_in[:, :, bass.ds(at + GA, U)]).then_inc(w_ok[j], 16)
                    sp.dma_start(wgb[j][:], w_in[:, :, bass.ds(at + GA + D, U)]).then_inc(w_ok[j], 16)
                    sp.dma_start(woa[j][:], out_a[:, :, bass.ds(at, U)]).then_inc(w_ok[j], 16)
                    sp.dma_start(wob[j][:], out_b[:, :, bass.ds(at, U)]).then_inc(w_ok[j], 16)

                for j in range(2):
                    load(j * U, j)
                with sp.Fori(1, UNITS // 2) as i:
                    for j in range(2):
                        sp.wait_ge(outs_ps, (2 * i - 1 + j) * PER)
                        load(i * (2 * U) + j * U, j)

            @block.tensor
            def _(pe):
                with pe.Fori(0, UNITS // 2) as i:
                    for j in range(2):
                        pe.wait_ge(w_ok[j], 64 * i + 64)
                        for c in range(2):
                            for n in range(PIECES):
                                r = c * PIECES + n
                                b = 4 * (r % 2)
                                cols, toks = slice(c * P, (c + 1) * P), slice(n * PIECE, (n + 1) * PIECE)
                                pe.wait_ge(free, (2 * i + j) * PER + r + 1)
                                for w, bank in ((wga[j], b), (wgb[j], b + 1)):
                                    for k in range(KD):
                                        last = pe.matmul(banks[bank][:, 0:PIECE], w[:, k, cols], hT[:, k, toks],
                                                         start=(k == 0), stop=(k == KD - 1))
                                last.then_inc(gates_ps, 1)
                                for w, y, bank in ((woa[j], yaT, b + 2), (wob[j], ybT, b + 3)):
                                    for k in range(CH):
                                        last = pe.matmul(banks[bank][:, 0:PIECE], w[:, k, cols], y[:, k, toks],
                                                         start=(k == 0), stop=(k == CH - 1))
                                last.then_inc(outs_ps, 1)

            @block.scalar
            def _(act):
                with act.Fori(0, UNITS) as i:
                    for r in range(PER):
                        b = 4 * (r % 2)
                        act.wait_ge(gates_ps, i * PER + r + 1)
                        act.wait_ge(free, i * PER + r + 1)
                        act.activation(sa[:, r % 2, :], banks[b][:, 0:PIECE], ACT.Sigmoid).then_inc(gates_ok, 1)
                        act.activation(sbb[:, r % 2, :], banks[b + 1][:, 0:PIECE], ACT.Sigmoid).then_inc(gates_ok, 1)

            @block.vector
            def _(dve):
                dve.sem_inc(free, 2)
                with dve.Fori(0, UNITS) as i:
                    for r in range(PER):
                        c, n = divmod(r, PIECES)
                        b = 4 * (r % 2)
                        dve.wait_ge(gates_ok, 2 * (i * PER + r) + 2)
                        dve.wait_ge(outs_ps, i * PER + r + 1)
                        dve.tensor_tensor(sa[:, r % 2, :], sa[:, r % 2, :], banks[b + 2][:, 0:PIECE], ALU.mult).then_inc(part, 1)
                        dve.tensor_tensor(sbb[:, r % 2, :], sbb[:, r % 2, :], banks[b + 3][:, 0:PIECE], ALU.mult).then_inc(part, 1)
                        dve.wait_ge(part, 2 * (i * PER + r) + 2)
                        dve.tensor_tensor(mT[:, bass.ds(2 * i + c, 1), n * PIECE:(n + 1) * PIECE].rearrange("p a n -> p (a n)"),
                                          sa[:, r % 2, :], sbb[:, r % 2, :], ALU.add).then_inc(free, 1)


def output_and_norm(nc, a, sb, sem, banks, ident, eps, mod_d, x2_d, xe_d, x_rows, mT, h2T):
    with ExitStack() as ctx:
        def tile(name, shape, dt=F32):
            return sb(name, shape, dt, ctx)

        wo = tile("wo", [P, KD, D])
        cond = tile("cond", [P, 3, D])
        cond_s = tile("cond_s", [NS, 3, D])
        gff = tile("gff", [P, D])
        xt = tile("xt", [P, 2, D])
        x2 = tile("x2", [P, 2, D])
        h2 = tile("h2", [P, 2, D])
        sqj = tile("sqj", [P, D])
        st = tile("st", [P, 4])
        names = "w4 c4 x4 mm4 x2ok sq4 r4 h4 st4 tp4 ev4 a4".split()
        wo_in, cond_in, _, mm, x2_ok, sq_ok, sd_ok, h2_ok, _, tp, ev, a_ok = (sem("s4" + n) for n in names)
        x_in = [sem("s4x0"), sem("s4x1")]
        stored = [sem("s4o0"), sem("s4o1")]
        dve4 = sem("dve4")
        with nc.Block() as block:
            @block.sync
            def _(sp):
                sp.dma_start(wo[:], a["w_o"].rearrange("l (k p) n -> p (l k) n", p=P)).then_inc(wo_in, 16)
                for j, m in enumerate((2, 4, 3)):
                    sp.dma_start(cond[:, j, :], mod_d[NS:NS + 1, m * D:(m + 1) * D].to_broadcast([P, D])).then_inc(cond_in, 16)
                    sp.dma_start(cond_s[:, j, :], mod_d[0:NS, m * D:(m + 1) * D]).then_inc(cond_in, 16)
                sp.dma_start(gff[:], a["norm_ffn_g"].to_broadcast([P, D])).then_inc(cond_in, 16)
                for t in range(TILES):
                    r = rows_of(t)
                    sp.wait_ge(x2_ok, t + 1)
                    sp.dma_start(x2_d[t * P:t * P + r, :], x2[0:r, t % 2, :]).then_inc(stored[t % 2], 16)
                    sp.wait_ge(h2_ok, t + 1)
                    sp.dma_start(xe_d[ROW0 + t * P:ROW0 + t * P + r, 0:D], h2[0:r, t % 2, :]).then_inc(stored[t % 2], 16)
                for b in range(2):
                    sp.wait_ge(stored[b], 32 * ((TILES + 1 - b) // 2))

            @block.gpsimd
            def _(pool):
                for t in range(TILES):
                    if t >= 2:
                        pool.wait_ge(x2_ok, t - 1)
                    pool.dma_start(xt[0:rows_of(t), t % 2, :], x_rows(t)).then_inc(x_in[t % 2], 16)

            @block.tensor
            def _(pe):
                pe.wait_ge(wo_in, 16)

                def product(t):
                    if t >= 2:
                        pe.wait_ge(x2_ok, t - 1)
                    r = rows_of(t)
                    for half in range(2):
                        for k in range(KD):
                            last = pe.matmul(banks[2 * (t % 2) + half][0:r, :], mT[:, k, t * P:t * P + r],
                                             wo[:, k, half * 512:(half + 1) * 512], start=(k == 0), stop=(k == KD - 1))
                    last.then_inc(mm, 1)

                def turn(t):
                    r = rows_of(t)
                    pe.wait_ge(h2_ok, t + 1)
                    if t >= 2:
                        pe.wait_ge(ev, 2 * t - 2)
                    for k in range(KD):
                        last = pe.transpose(banks[4 + 2 * (t % 2) + k // 4][:, (k % 4) * P:(k % 4) * P + r],
                                            h2[0:r, t % 2, k * P:(k + 1) * P], ident[0:r, 0:r])
                    last.then_inc(tp, 1)

                product(0)
                for t in range(TILES):
                    if t + 1 < TILES:
                        product(t + 1)
                    turn(t)

            @block.scalar
            def _(act):
                def square(t):
                    r = rows_of(t)
                    act.wait_ge(x2_ok, t + 1)
                    if t:
                        act.wait_ge(h2_ok, t)
                    act.activation(sqj[0:r, :], x2[0:r, t % 2, :], ACT.Square, accum_out=st[0:r, 0:1]).then_inc(sq_ok, 1)
                    act.wait_ge(sq_ok, t + 1)
                    act.activation(st[0:r, 1:2], st[0:r, 0:1], ACT.Sqrt, scale=1.0 / D, bias=eps[0:r, 0:1]).then_inc(sd_ok, 1)

                def take(t):
                    r = rows_of(t)
                    act.wait_ge(tp, t + 1)
                    for half in range(2):
                        act.activation(h2T[:, 4 * half:4 * half + 4, t * P:t * P + r],
                                       banks[4 + 2 * (t % 2) + half][:].rearrange("p (k n) -> p k n", n=P)[:, :, 0:r],
                                       ACT.Copy).then_inc(ev, 1)

                for t in range(TILES):
                    square(t)
                    take(t)

            @block.vector
            def _(dve):
                s = Steps(dve, dve4)
                dve.wait_ge(cond_in, 16 * 7)
                s.run(dve.scalar_tensor_tensor(out=cond[:, 1, :], in0=cond[:, 1, :], scalar=1.0, in1=gff[:], op0=ALU.add, op1=ALU.mult))
                s.run(dve.scalar_tensor_tensor(out=cond_s[:, 1, :], in0=cond_s[:, 1, :], scalar=1.0, in1=gff[0:NS, :], op0=ALU.add, op1=ALU.mult))
                s.settle()
                for t in range(TILES):
                    r = rows_of(t)
                    c = (cond if t < TILES - 1 else cond_s)[0:r]
                    dve.wait_ge(mm, t + 1)
                    dve.wait_ge(x_in[t % 2], 16 * (t // 2 + 1))
                    if t >= 2:
                        dve.wait_ge(stored[t % 2], 32 * (t // 2))
                    for half in range(2):
                        at = slice(512 * half, 512 * half + 512)
                        s.run(dve.tensor_tensor(x2[0:r, t % 2, at], banks[2 * (t % 2) + half][0:r, :], c[:, 0, at], ALU.mult))
                    s.settle()
                    dve.tensor_tensor(x2[0:r, t % 2, :], x2[0:r, t % 2, :], xt[0:r, t % 2, :], ALU.add).then_inc(x2_ok, 1)
                    dve.wait_ge(sd_ok, t + 1)
                    s.link(dve.reciprocal(st[0:r, 2:3], st[0:r, 1:2]))
                    if t >= 2:
                        dve.wait_ge(tp, t - 1)
                    s.link(dve.scalar_tensor_tensor(out=h2[0:r, t % 2, :], in0=x2[0:r, t % 2, :], scalar=st[0:r, 2:3],
                                                    in1=c[:, 1, :], op0=ALU.mult, op1=ALU.mult))
                    dve.tensor_tensor(h2[0:r, t % 2, :], h2[0:r, t % 2, :], c[:, 2, :], ALU.add).then_inc(h2_ok, 1)


def routing(nc, a, sb, sem, banks, hT, xe_d, acc_d, posm, table, total, tok, idle, iota, wexp, slot_in):
    with ExitStack() as ctx:
        def tile(name, shape, dt=F32):
            return sb(name, shape, dt, ctx)

        wr = tile("wr", [P, KD, E])
        wsh = tile("wsh", [P, KD, 2 * FF])
        wsd = tile("wsd", [P, FF // P, D])
        sg = tile("sgs", [P, 2, PIECE])
        hs = tile("hs", [P, FF // P, TT])
        ysh = tile("ysh", [P, 2, D])
        zero = tile("zero", [P, XW // 2])
        rb = tile("rb", [P, E])
        sc = tile("sc", [P, TILES, E])
        sel = tile("selr", [P, TILES, E])
        top8 = tile("top8", [P, TILES * EG, 8])
        gs = tile("gs", [P, TILES, EG])
        gt = tile("gt", [P, TILES, EG, EG])
        eq = tile("eq", [P, TILES, EG, EG])
        lower = tile("lower", [P, EG, EG])
        gok = tile("gok", [P, TILES, EG])
        pen = tile("pen", [P, TILES, EG])
        mask = tile("mask", [P, TILES, E])
        maskb = tile("maskb", [P, TILES, E], BF16)
        wsum = tile("wsum", [P, TILES])
        wts = eq[:].rearrange("p t a b -> p t (a b)")
        base = gt[:].rearrange("p t a b -> p t (a b)")
        tri = tile("tri", [P, P], BF16)
        trii = tile("trii", [P, P], BF16)
        onesb = tile("onesb", [P, P], BF16)
        thr = tile("thr", [P, 8])
        thj = tile("thj", [E, 8])
        nb = tile("nb", [E, 4])
        nbb = tile("nbb", [E, 2], BF16)
        past = tile("past", [E, ITEMS + AHEAD], BF16)
        tf = tile("tf", [1, 2, ITEMS + AHEAD])
        names = ("w_in b_in lg sc mk pf tot cnt nb incl past tab wt const z "
                 "gps gok ups hok dps yok").split()
        (w_ok, rb_ok, lg_ps, sc_ok, mk_ok, pf_ps, _, cnt_ps, nb_ok, incl_ps, past_ok, tab_ps, wt_ok, const_ok, z_ok,
         g_ps, g_ok, u_ps, h_ok, d_ps, y_ok) = (sem("s5" + n) for n in names)
        dve5, pool5 = sem("dve5"), sem("pool5")
        stored = [sem("s5y0"), sem("s5y1"), sem("s5w")]
        sh_in = sem("s5sh")
        pieces = [(f, n) for f in range(FF // P) for n in range(PIECES)]
        FULL = TILES - 1
        with nc.Block() as block:
            @block.sync
            def _(sp):
                sp.dma_start(wr[:], a["w_router"].rearrange("l (k p) n -> p (l k) n", p=P)).then_inc(w_ok, 16)
                sp.dma_start(rb[:], a["router_bias"].to_broadcast([P, E])).then_inc(rb_ok, 16)
                sp.dma_start(wsh[:, :, 0:FF], a["w_sh_gate"].rearrange("l (k p) n -> p (l k) n", p=P)).then_inc(sh_in, 16)
                sp.dma_start(wsh[:, :, FF:], a["w_sh_up"].rearrange("l (k p) n -> p (l k) n", p=P)).then_inc(sh_in, 16)
                sp.dma_start(wsd[:], a["w_sh_down"].rearrange("l (k p) n -> p (l k) n", p=P)).then_inc(sh_in, 16)
                for e in range(2):
                    load_expert(sp, a, wexp, e, e, slot_in[e])
                sp.wait_ge(z_ok, 1)
                for c in range(2):
                    sp.dma_start(xe_d[0:ROW0, c * (XW // 2):(c + 1) * (XW // 2)], zero[0:ROW0, :]).then_inc(stored[2], 16)
                    sp.dma_start(acc_d[0:ROW0, c * (D // 2):(c + 1) * (D // 2)], zero[0:ROW0, 0:D // 2]).then_inc(stored[2], 16)
                    sp.dma_start(xe_d[ROW0 + TT:, c * (XW // 2):(c + 1) * (XW // 2)], zero[:]).then_inc(stored[2], 16)
                sp.wait_ge(wt_ok, 1)
                for t in range(TILES):
                    r = rows_of(t)
                    sp.dma_start(xe_d[ROW0 + t * P:ROW0 + t * P + r, D:], wts[0:r, t, :]).then_inc(stored[2], 16)
                for t in range(TILES):
                    r = rows_of(t)
                    sp.wait_ge(y_ok, 2 * t + 2)
                    sp.dma_start(acc_d[ROW0 + t * P:ROW0 + t * P + r, :], ysh[0:r, t % 2, :]).then_inc(stored[t % 2], 16)
                sp.wait_ge(stored[2], 16 * (TILES + 6))
                for b in range(2):
                    sp.wait_ge(stored[b], 16 * ((TILES + 1 - b) // 2))

            @block.gpsimd
            def _(pool):
                pool.memset(zero[:], 0.0).then_inc(z_ok, 1)
                pool.memset(tri[:], 1.0).then_inc(pool5, 1)
                pool.memset(trii[:], 1.0).then_inc(pool5, 1)
                pool.memset(lower[:], 1.0).then_inc(pool5, 1)
                pool.memset(onesb[:], 1.0).then_inc(const_ok, 1)
                pool.memset(posm[:], -1.0).then_inc(const_ok, 1)
                pool.memset(mask[:, FULL, :], 0.0).then_inc(const_ok, 1)
                pool.memset(sc[:, FULL, :], 0.0).then_inc(const_ok, 1)
                pool.iota(iota[:], [[1, TILES * P]], base=0, channel_multiplier=0,
                          allow_small_or_imprecise_dtypes=True).then_inc(const_ok, 1)
                pool.iota(idle[:], [[0, 1]], base=ROW0 + TT, channel_multiplier=1,
                          allow_small_or_imprecise_dtypes=True).then_inc(const_ok, 1)
                pool.iota(tok[:, :, 0:1], [[0, TILES], [0, 1]], base=ROW0, channel_multiplier=1,
                          allow_small_or_imprecise_dtypes=True).then_inc(const_ok, 1)
                pool.iota(tok[:, :, 1:2], [[P, TILES], [0, 1]], base=0, channel_multiplier=0,
                          allow_small_or_imprecise_dtypes=True).then_inc(const_ok, 1)
                pool.iota(thr[:], [[P, 8]], base=P, channel_multiplier=0,
                          allow_small_or_imprecise_dtypes=True).then_inc(const_ok, 1)
                pool.wait_ge(pool5, 3)
                pool.affine_select(out=tri[:], in_=tri[:], compare_op=ALU.is_gt, fill=0.0, base=0,
                                   pattern=[[1, P]], channel_multiplier=-1).then_inc(const_ok, 1)
                pool.affine_select(out=trii[:], in_=trii[:], compare_op=ALU.is_ge, fill=0.0, base=0,
                                   pattern=[[1, P]], channel_multiplier=-1).then_inc(const_ok, 1)
                pool.affine_select(out=lower[:], in_=lower[:], compare_op=ALU.is_gt, fill=0.0, base=0,
                                   pattern=[[1, EG], [-1, EG]], channel_multiplier=0).then_inc(const_ok, 1)
                for r, (f, n) in enumerate(pieces):
                    pool.wait_ge(g_ok, 2 * r + 2)
                    at = hs[:, f, n * PIECE:(n + 1) * PIECE]
                    pool.tensor_tensor(at, at, sg[:, r % 2, :], ALU.mult).then_inc(h_ok, 1)

            CONST = 12

            @block.tensor
            def _(pe):
                pe.wait_ge(w_ok, 16)
                for t in range(TILES):
                    r = rows_of(t)
                    bank, at = (0, t * E) if t < 5 else (1, (t - 5) * E)
                    for k in range(KD):
                        last = pe.matmul(banks[bank][0:r, at:at + E], hT[:, k, t * P:t * P + r], wr[:, k, :],
                                         start=(k == 0), stop=(k == KD - 1))
                last.then_inc(lg_ps, 1)
                pe.wait_ge(sh_in, 48)
                for r, (f, n) in enumerate(pieces):
                    toks = slice(n * PIECE, (n + 1) * PIECE)
                    if r >= 1:
                        pe.wait_ge(g_ok, 2 * r)
                    for half in range(2):
                        for k in range(KD):
                            last = pe.matmul(banks[2 + half][:, 0:PIECE], wsh[:, k, half * FF + f * P:half * FF + (f + 1) * P],
                                             hT[:, k, toks], start=(k == 0), stop=(k == KD - 1))
                    last.then_inc(g_ps, 1)
                pe.wait_ge(const_ok, CONST)
                pe.wait_ge(mk_ok, 1)
                pe.matmul(banks[0][:], tri[:], maskb[:, 0:FULL, :].rearrange("p t e -> p (t e)"), start=True, stop=True)
                pe.matmul(banks[4][0:NS, 0:E], tri[0:NS, 0:NS], maskb[0:NS, FULL, :], start=True, stop=True)
                pe.matmul(banks[1][:], onesb[:], maskb[:, 0:FULL, :].rearrange("p t e -> p (t e)"), start=True,
                          stop=True).then_inc(pf_ps, 1)
                for t in range(TILES):
                    last = pe.matmul(banks[5][0:E, 0:1], maskb[:, t, :], onesb[:, 0:1], start=(t == 0), stop=(t == TILES - 1))
                last.then_inc(cnt_ps, 1)
                pe.wait_ge(nb_ok, 1)
                pe.matmul(banks[6][0:E, 0:1], trii[0:E, 0:E], nbb[:, 0:1], start=True, stop=True).then_inc(incl_ps, 1)
                pe.wait_ge(past_ok, 1)
                n = ITEMS + AHEAD
                pe.matmul(banks[7][0:1, 0:n], onesb[0:E, 0:1], past[:], start=True, stop=True)
                pe.matmul(banks[7][0:1, 256:256 + n], nbb[:, 0:1], past[:], start=True, stop=True)
                pe.matmul(banks[7][0:1, 500:501], nbb[:, 0:1], onesb[0:E, 0:1], start=True, stop=True).then_inc(tab_ps, 1)
                pe.wait_ge(h_ok, len(pieces))
                for t in range(TILES):
                    r = rows_of(t)
                    for half in range(2):
                        if t >= 1:
                            pe.wait_ge(y_ok, 2 * t - 1 + half)
                        for f in range(FF // P):
                            last = pe.matmul(banks[2 + half][0:r, :], hs[:, f, t * P:t * P + r],
                                             wsd[:, f, half * 512:(half + 1) * 512], start=(f == 0), stop=(f == FF // P - 1))
                        last.then_inc(d_ps, 1)

            @block.scalar
            def _(act):
                act.wait_ge(const_ok, CONST)
                act.wait_ge(lg_ps, 1)
                act.activation(sc[:, 0:5, :].rearrange("p t e -> p (t e)"), banks[0][:, 0:5 * E], ACT.Sigmoid).then_inc(sc_ok, 1)
                act.activation(sc[:, 5:FULL, :].rearrange("p t e -> p (t e)"), banks[1][:, 0:3 * E], ACT.Sigmoid).then_inc(sc_ok, 1)
                act.activation(sc[0:NS, FULL, :], banks[1][0:NS, 3 * E:4 * E], ACT.Sigmoid).then_inc(sc_ok, 1)
                for r, (f, n) in enumerate(pieces):
                    act.wait_ge(g_ps, r + 1)
                    if r >= 2:
                        act.wait_ge(h_ok, r - 1)
                    act.activation(sg[:, r % 2, :], banks[2][:, 0:PIECE], ACT.Silu).then_inc(g_ok, 1)
                    act.activation(hs[:, f, n * PIECE:(n + 1) * PIECE], banks[3][:, 0:PIECE], ACT.Copy).then_inc(g_ok, 1)
                for t in range(TILES):
                    r = rows_of(t)
                    if t >= 2:
                        act.wait_ge(stored[t % 2], 16 * (t // 2))
                    for half in range(2):
                        act.wait_ge(d_ps, 2 * t + half + 1)
                        act.activation(ysh[0:r, t % 2, half * 512:(half + 1) * 512], banks[2 + half][0:r, :],
                                       ACT.Copy).then_inc(y_ok, 1)

            @block.vector
            def _(dve):
                s = Steps(dve, dve5)
                dve.wait_ge(rb_ok, 16)
                dve.wait_ge(sc_ok, 3)
                dve.wait_ge(const_ok, CONST)
                s.link(dve.tensor_tensor(sel[:], sc[:], rb[:].unsqueeze(1).to_broadcast([P, TILES, E]), ALU.add))
                for t in range(TILES):
                    for g in range(EG):
                        s.run(dve.max(top8[:, t * EG + g, :], sel[:, t, g * EG:(g + 1) * EG]))
                s.settle()
                s.link(dve.tensor_tensor(gs[:].rearrange("p t g -> p (t g)"), top8[:, :, 0], top8[:, :, 1], ALU.add))
                this = gs[:].unsqueeze(3).to_broadcast([P, TILES, EG, EG])
                other = gs[:].unsqueeze(2).to_broadcast([P, TILES, EG, EG])
                s.run(dve.tensor_tensor(gt[:], other, this, ALU.is_gt))
                s.link(dve.tensor_tensor(eq[:], other, this, ALU.is_equal))
                s.link(dve.tensor_tensor(eq[:], eq[:], lower[:].unsqueeze(1).to_broadcast([P, TILES, EG, EG]), ALU.mult))
                s.link(dve.tensor_tensor(gt[:], gt[:], eq[:], ALU.add))
                s.link(dve.tensor_reduce(pen[:], gt[:], AX.X, ALU.add))
                s.link(dve.tensor_scalar(gok[:], pen[:], float(TOPG), None, ALU.is_lt))
                s.link(dve.tensor_scalar(pen[:], gok[:], -NEG, NEG, ALU.mult, ALU.add))
                sel4 = sel[:].rearrange("p t (g e) -> p t g e", e=EG)
                s.link(dve.tensor_tensor(sel4, sel4, gok[:].unsqueeze(3).to_broadcast([P, TILES, EG, EG]), ALU.mult))
                s.link(dve.tensor_tensor(sel4, sel4, pen[:].unsqueeze(3).to_broadcast([P, TILES, EG, EG]), ALU.add))
                for t in range(TILES):
                    s.run(dve.max(top8[:, t, :], sel[:, t, :]))
                s.settle()
                for t in range(TILES):
                    s.run(dve.match_replace(wts[:, t, :], top8[:, t, :], sel[:, t, :], 2 * NEG))
                s.settle()
                s.run(dve.tensor_scalar(mask[:, 0:FULL, :], wts[:, 0:FULL, :], 1.5 * NEG, None, ALU.is_lt))
                s.link(dve.tensor_scalar(mask[0:NS, FULL, :], wts[0:NS, FULL, :], 1.5 * NEG, None, ALU.is_lt))
                dve.tensor_copy(maskb[:], mask[:]).then_inc(mk_ok, 1)
                s.link(dve.tensor_tensor(wts, sc[:], mask[:], ALU.mult))
                s.run(dve.tensor_reduce(wsum[:, 0:FULL], wts[:, 0:FULL, :], AX.X, ALU.add))
                s.link(dve.tensor_reduce(wsum[0:NS, FULL:], wts[0:NS, FULL:, :], AX.X, ALU.add))
                s.run(dve.reciprocal(wsum[:, 0:FULL], wsum[:, 0:FULL]))
                s.link(dve.reciprocal(wsum[0:NS, FULL:], wsum[0:NS, FULL:]))
                s.run(dve.tensor_scalar(wsum[:, 0:FULL], wsum[:, 0:FULL], SCALE, None, ALU.mult))
                s.link(dve.tensor_scalar(wsum[0:NS, FULL:], wsum[0:NS, FULL:], SCALE, None, ALU.mult))
                s.run(dve.tensor_tensor(wts[:, 0:FULL, :], wts[:, 0:FULL, :],
                                        wsum[:, 0:FULL].unsqueeze(2).to_broadcast([P, FULL, E]), ALU.mult))
                s.link(dve.tensor_scalar(wts[0:NS, FULL, :], wts[0:NS, FULL, :], wsum[0:NS, FULL:], None, ALU.mult))
                dve.sem_inc(wt_ok, 1)
                s.run(dve.memset(base[:, 0, :], 0.0))
                dve.wait_ge(pf_ps, 1)
                for t in range(1, TILES):
                    s.settle()
                    s.run(dve.tensor_tensor(base[:, t, :], base[:, t - 1, :], banks[1][:, (t - 1) * E:t * E], ALU.add))
                s.settle()
                s.run(dve.tensor_tensor(base[:, 0:FULL, :], base[:, 0:FULL, :],
                                        banks[0][:].rearrange("p (t e) -> p t e", e=E), ALU.add))
                s.link(dve.tensor_tensor(base[0:NS, FULL, :], base[0:NS, FULL, :], banks[4][0:NS, 0:E], ALU.add))
                s.run(dve.scalar_tensor_tensor(out=base[:, 0:FULL, :], in0=base[:, 0:FULL, :], scalar=1.0,
                                               in1=mask[:, 0:FULL, :], op0=ALU.add, op1=ALU.mult))
                s.link(dve.scalar_tensor_tensor(out=base[0:NS, FULL, :], in0=base[0:NS, FULL, :], scalar=1.0,
                                                in1=mask[0:NS, FULL, :], op0=ALU.add, op1=ALU.mult))
                s.run(dve.tensor_scalar(posm[:, 0:E, 0:FULL], base[:, 0:FULL, :].rearrange("p t e -> p e t"), -1.0, None, ALU.add))
                s.run(dve.tensor_scalar(posm[0:NS, 0:E, FULL], base[0:NS, FULL, :], -1.0, None, ALU.add))
                dve.wait_ge(cnt_ps, 1)
                s.link(dve.tensor_copy(nb[:, 0:1], banks[5][0:E, 0:1]))
                s.link(dve.tensor_scalar(thj[:], thr[0:E, :], nb[:, 0:1], None, ALU.is_lt))
                s.link(dve.tensor_reduce(nb[:, 1:2], thj[:], AX.X, ALU.add))
                dve.tensor_scalar(nbb[:, 0:1], nb[:, 1:2], 1.0, None, ALU.add).then_inc(nb_ok, 1)
                dve.wait_ge(incl_ps, 1)
                s.link(dve.tensor_copy(nb[:, 2:3], banks[6][0:E, 0:1]))
                dve.tensor_scalar(past[:], iota[0:E, 0:ITEMS + AHEAD], nb[:, 2:3], None, ALU.is_ge).then_inc(past_ok, 1)
                dve.wait_ge(tab_ps, 1)
                n = ITEMS + AHEAD
                s.run(dve.tensor_copy(table[:, :, 0], banks[7][0:1, 0:n]))
                s.run(dve.tensor_copy(total[:], banks[7][0:1, 500:501]))
                s.link(dve.tensor_tensor(tf[:, 0, :], iota[0:1, 0:n], banks[7][0:1, 256:256 + n], ALU.subtract))
                s.link(dve.tensor_scalar(tf[:, 1, :], tf[:, 0, :], float(TILES - 1), float(P), ALU.min, ALU.mult))
                s.link(dve.tensor_scalar(tf[:, 0, :], banks[7][0:1, 0:n], float(E), float(P), ALU.is_ge, ALU.mult))
                s.link(dve.tensor_tensor(tf[:, 1, :], tf[:, 1, :], tf[:, 0, :], ALU.max))
                s.link(dve.tensor_copy(table[:, :, 1], tf[:, 1, :]))


def load_expert(eng, a, wexp, e, slot, landed):
    def src(name):
        return a[name][0, bass.ds(e, 1)].rearrange("e (k p) n -> p (e k) n", p=P)

    eng.dma_start(wexp[:, slot, 0:KD, 0:FF], src("w_exp_gate")).then_inc(landed, 16)
    eng.dma_start(wexp[:, slot, 0:KD, FF:], src("w_exp_up")).then_inc(landed, 16)
    eng.dma_start(wexp[:, slot, KD:, :].rearrange("p (k h) n -> p k (h n)", h=2), src("w_exp_down")).then_inc(landed, 16)


def experts(nc, a, sb, sem, banks, ident, xe_d, acc_d, posm, table, total, tok, idle, iota, wexp, slot_in):
    with ExitStack() as ctx:
        def tile(name, shape, dt=F32):
            return sb(name, shape, dt, ctx)

        xg = tile("xg", [P, 2, XW + 1])
        xT = tile("xT", [P, 2, KD, P])
        oh = tile("oh", [P, 2, TILES, P], BF16)
        sg = tile("sg", [P, FF])
        hh = tile("hh", [P, FF])
        hT = tile("hTe", [P, FF // P, P])
        ob = tile("ob", [P, 2, D])
        wcol = tile("wcol", [P, 2])
        none = tile("none", [P, D // 2])
        ixf = tile("ixf", [P, 4])
        lists = tile("lists", [P, LISTS], U32)
        ix = [tile(f"ix{b}", [P, 1], U32) for b in range(2)]
        ixs = [tile(f"ixs{b}", [P, 1], U32) for b in range(2)]
        names = "oh ixp ls ix ixs tp xT wc gu sg h hp hT dn ob scat w ent pad fin".split()
        (oh_ok, ix_ps, list_ok, ix_ok, ixs_ok, x_tp, xT_ok, wc_ok, gu_ps, sg_ok, h_ok, h_tp, hT_ok, dn_ps, ob_ok, added,
         w_ok, entered, pad_ok, _) = (sem("s6" + n) for n in names)
        gat = [sem("s6g0"), sem("s6g1")]
        passed = sem("s6passed")
        dve6 = sem("dve6")

        def entry(eng, i, field, top):
            return eng.value_load(table[0:1, bass.ds(i, 1), field:field + 1].rearrange("a b c -> a (b c)"),
                                  min_val=0, max_val=top)

        def blocks(eng, body, enter=None, leave=None):
            with eng.Fori(0, ITEMS // SPAN) as span:
                with eng.If(entry(eng, span * SPAN, 0, E) < E):
                    with eng.Fori(0, SPAN // 2) as part:
                        it = span * (SPAN // 2) + part
                        if enter:
                            enter(it)
                        for b in range(2):
                            i = it * 2 + b
                            with eng.If(entry(eng, i, 0, E) < E):
                                body(i, b)
                            eng.nop()
                    eng.nop()
                eng.nop()
            if leave:
                leave()

        def round_of(i, b):
            return (i - b) * 8

        with nc.Block() as block:
            @block.sync
            def _(sp):
                def turn(e, slot, first=False):
                    if not first:
                        sp.wait_ge(entered, e - 1)
                    load_expert(sp, a, wexp, e, slot, slot_in[slot])

                def land(e, slot, round_):
                    sp.wait_ge(slot_in[slot], 48 * round_ + 48)
                    sp.sem_inc(w_ok, 1)

                turn(2, 2, True)
                land(0, 0, 0)
                land(1, 1, 0)
                turn(3, 3, True)
                land(2, 2, 0)
                with sp.Fori(1, E // RING) as r:
                    for j in range(RING):
                        turn(r * RING + j, j)
                        land(r * RING + j - 1, (j - 1) % RING, r if j else r - 1)
                land(E - 1, RING - 1, E // RING - 1)

            @block.gpsimd
            def _(pool):
                pool.memset(xg[:, :, XW:XW + 1], 0.0).then_inc(pad_ok, 1)
                pool.memset(none[:], 0.0).then_inc(pad_ok, 1)
                pool.wait_ge(pad_ok, 2)
                for c in range(2):
                    pool.dma_start(acc_d[ROW0 + TT:, c * (D // 2):(c + 1) * (D // 2)], none[:]).then_inc(added, 16)

                def gather(j, b):
                    pool.wait_ge(ix_ok, j + 1)
                    pool.sem_inc(passed, 1)
                    pool.indirect_dma_start(out=xg[:, b, 0:XW], out_offset=None, in_=xe_d,
                                            in_offset=bass.IndirectOffsetOnAxis(ap=ix[b][:, 0:1], axis=0)).then_inc(gat[b], 16)

                gather(0, 0)
                gather(1, 1)
                pool.wait_ge(x_tp, 1)
                pool.wait_ge(wc_ok, 1)
                gather(2, 0)

                def block_of(i, b):
                    pool.wait_ge(x_tp, i + 2)
                    pool.wait_ge(wc_ok, i + 2)
                    gather(i + 3, 1 - b)
                    pool.wait_ge(ob_ok, 2 * i + 4)
                    pool.wait_ge(ixs_ok, i + 1)
                    pool.wait_ge(added, 16 * i + 32)
                    pool.sem_inc(passed, 1)
                    pool.indirect_dma_start(out=acc_d, out_offset=bass.IndirectOffsetOnAxis(ap=ixs[b][:, 0:1], axis=0),
                                            in_=ob[:, b, :], in_offset=None, compute_op=ALU.add).then_inc(added, 16)

                blocks(pool, block_of)
                n = pool.value_load(total[0:1, 0:1], min_val=E, max_val=ITEMS)
                pool.wait_ge(added, 16 * n + 32)
                pool.wait_ge(gat[0], 16 * ((n + 4) // 2))
                pool.wait_ge(gat[1], 16 * ((n + 3) // 2))

            @block.tensor
            def _(pe):
                def index(j, b, later=True):
                    pe.wait_ge(oh_ok, j + 1)
                    if later:
                        pe.wait_ge(list_ok, j - 1)
                    for t in range(TILES):
                        last = pe.matmul(banks[6 + b][:, 0:2], oh[:, b, t, :], tok[:, t, :], start=(t == 0),
                                         stop=(t == TILES - 1))
                    last.then_inc(ix_ps, 1)

                def turn(j, b, landed):
                    pe.wait_ge(gat[b], landed)
                    if j is not 0:
                        pe.wait_ge(xT_ok, 2 * j)
                    for k in range(KD):
                        last = pe.transpose(banks[1 + k // 4][:, (k % 4) * P:(k % 4 + 1) * P], xg[:, b, k * P:(k + 1) * P],
                                            ident[:])
                    last.then_inc(x_tp, 1)

                def up(j, b, e, c):
                    slot = e & (RING - 1)

                    def part(k):
                        return pe.matmul(banks[0][:], xT[:, b, k, :],
                                         wexp[:, bass.ds(slot, 1), k, :].rearrange("p a n -> p (a n)"),
                                         start=(k == 0), stop=(k == KD - 1))

                    pe.wait_ge(xT_ok, 2 * j + 2)
                    with pe.If(c < 1):
                        pe.wait_ge(w_ok, e + 1)
                        part(0).then_inc(entered, 1)
                    with pe.Else():
                        part(0)
                    for k in range(1, KD):
                        last = part(k)
                    last.then_inc(gu_ps, 1)

                index(0, 0, False)
                index(1, 1, False)
                turn(0, 0, 16)
                index(2, 0)
                turn(1, 1, 16)
                index(3, 1)
                pe.sem_inc(ob_ok, 2)
                up(0, 0, entry(pe, 0, 0, E), entry(pe, 0, 1, (TILES - 1) * P))

                def block_of(i, b):
                    e = entry(pe, i, 0, E)
                    pe.wait_ge(h_ok, i + 1)
                    for f in range(FF // P):
                        last = pe.transpose(banks[3][:, f * P:(f + 1) * P], hh[:, f * P:(f + 1) * P], ident[:])
                    last.then_inc(h_tp, 1)
                    up(i + 1, 1 - b, entry(pe, i + 1, 0, E), entry(pe, i + 1, 1, (TILES - 1) * P))
                    index(i + 4, b)
                    turn(i + 2, b, round_of(i, b) + 32)
                    slot = e & (RING - 1)
                    pe.wait_ge(hT_ok, i + 1)
                    pe.wait_ge(ob_ok, 2 * i + 2)
                    for half in range(2):
                        for f in range(FF // P):
                            last = pe.matmul(banks[4 + half][:], hT[:, f, :],
                                             wexp[:, bass.ds(slot, 1), KD + 2 * f + half, :].rearrange("p a n -> p (a n)"),
                                             start=(f == 0), stop=(f == FF // P - 1))
                    last.then_inc(dn_ps, 1)

                blocks(pe, block_of)

            @block.scalar
            def _(act):
                def take(j, b):
                    act.wait_ge(x_tp, j + 1)
                    act.wait_ge(gu_ps, j - 1) if j is not 0 and j is not 1 else None
                    act.activation(xT[:, b, 0:4, :].rearrange("p k n -> p (k n)"), banks[1][:], ACT.Copy).then_inc(xT_ok, 1)

                def gate(j):
                    act.wait_ge(gu_ps, j + 1)
                    act.activation(sg[:], banks[0][:, 0:FF], ACT.Silu).then_inc(sg_ok, 1)

                take(0, 0)
                take(1, 1)
                gate(0)

                def block_of(i, b):
                    act.wait_ge(h_tp, i + 1)
                    act.activation(hT[:].rearrange("p f n -> p (f n)"), banks[3][:, 0:FF], ACT.Copy).then_inc(hT_ok, 1)
                    gate(i + 1)
                    take(i + 2, b)
                    act.wait_ge(dn_ps, i + 1)
                    act.wait_ge(ixs_ok, i + 1)
                    act.activation(ob[:, b, 0:512], banks[4][:], ACT.Copy, scale=wcol[:, b:b + 1]).then_inc(ob_ok, 1)

                blocks(act, block_of)

            @block.vector
            def _(dve):
                s = Steps(dve, dve6)

                def place(j, b):
                    e = entry(dve, j, 0, E)
                    c = entry(dve, j, 1, (TILES - 1) * P)
                    dve.tensor_tensor(oh[:, b, :, :], iota[:, bass.ds(c, P)].unsqueeze(1).to_broadcast([P, TILES, P]),
                                      posm[:, bass.ds(e, 1), :].rearrange("p a t -> p (a t)").unsqueeze(2).to_broadcast([P, TILES, P]),
                                      ALU.is_equal).then_inc(oh_ok, 1)

                def index(j, b):
                    dve.wait_ge(ix_ps, j + 1)
                    s.link(dve.tensor_copy(ixf[:, 0:2], banks[6 + b][:, 0:2]))
                    s.link(dve.tensor_tensor(ixf[:, 2:3], ixf[:, 0:1], ixf[:, 1:2], ALU.add))
                    s.link(dve.scalar_tensor_tensor(out=ixf[:, 3:4], in0=ixf[:, 2:3], scalar=0.0, in1=idle[:], op0=ALU.is_equal,
                                                    op1=ALU.mult))
                    dve.tensor_tensor(lists[:, bass.ds(j & (LISTS - 1), 1)], ixf[:, 2:3], ixf[:, 3:4], ALU.add).then_inc(list_ok, 1)

                def take(j, b):
                    dve.wait_ge(x_tp, j + 1)
                    dve.tensor_copy(xT[:, b, 4:8, :].rearrange("p k n -> p (k n)"), banks[2][:]).then_inc(xT_ok, 1)

                def weight(j, b, e, landed):
                    dve.wait_ge(gat[b], landed)
                    dve.tensor_copy(wcol[:, b:b + 1], xg[:, b, bass.ds(e + D, 1)]).then_inc(wc_ok, 1)

                def gate(j):
                    dve.wait_ge(sg_ok, j + 1)
                    dve.tensor_tensor(hh[:], sg[:], banks[0][:, FF:], ALU.mult).then_inc(h_ok, 1)

                def to_gather(j, b):
                    dve.wait_ge(list_ok, j + 1)
                    dve.tensor_copy(ix[b][:], lists[:, bass.ds(j & (LISTS - 1), 1)]).then_inc(ix_ok, 1)

                def to_add(j, b):
                    dve.tensor_copy(ixs[b][:], lists[:, bass.ds(j & (LISTS - 1), 1)]).then_inc(ixs_ok, 1)

                dve.wait_ge(pad_ok, 2)
                for j in range(2):
                    place(j, j)
                for j in range(2):
                    index(j, j)
                    to_gather(j, j)
                take(0, 0)
                weight(0, 0, entry(dve, 0, 0, E), 16)
                place(2, 0)
                index(2, 0)
                to_gather(2, 0)
                place(3, 1)
                take(1, 1)
                weight(1, 1, entry(dve, 1, 0, E), 16)
                index(3, 1)
                gate(0)

                def block_of(i, b):
                    dve.wait_ge(gat[1 - b], round_of(i, b) + 16 + 16 * b)
                    to_gather(i + 3, 1 - b)
                    place(i + 4, b)
                    gate(i + 1)
                    dve.wait_ge(gu_ps, i + 2)
                    take(i + 2, b)
                    dve.wait_ge(added, 16 * i + 16)
                    to_add(i, b)
                    index(i + 4, b)
                    dve.wait_ge(dn_ps, i + 1)
                    dve.tensor_scalar(ob[:, b, 512:], banks[5][:], wcol[:, b:b + 1], None, ALU.mult).then_inc(ob_ok, 1)
                    dve.wait_ge(ob_ok, 2 * i + 4)
                    weight(i + 2, b, entry(dve, i + 2, 0, E), round_of(i, b) + 32)

                blocks(dve, block_of, lambda it: s.enter(it, 2 * 3), lambda: s.leave(ITEMS // 2))


def final(nc, a, o, sb, sem, eps, mod_d, x2_d, acc_d):
    with ExitStack() as ctx:
        def tile(name, shape, dt=F32):
            return sb(name, shape, dt, ctx)

        g2 = tile("g2", [P, D])
        g2s = tile("g2s", [NS, D])
        fg = tile("fg", [P, D])
        xx = tile("xx", [P, 4, D])
        aa = tile("aa", [P, 4, D])
        yy = tile("yy", [P, 2, D])
        sqj = tile("sqf", [P, D])
        st = tile("stf", [P, 4])
        c_in, sum_ok, sq_ok, sd_ok, y_ok = (sem("s7" + n) for n in "c sum sq sd y".split())
        t_in = [sem(f"s7i{j}") for j in range(4)]
        out = [sem(f"s7o{j}") for j in range(2)]
        dve7 = sem("dve7")
        y_p = o["y_prompt"].rearrange("b t d -> (b t) d")
        y_s = o["y_sample"].rearrange("b t d -> (b t) d")
        with nc.Block() as block:
            @block.sync
            def _(sp):
                sp.dma_start(g2[:], mod_d[NS:NS + 1, 5 * D:].to_broadcast([P, D])).then_inc(c_in, 16)
                sp.dma_start(g2s[:], mod_d[0:NS, 5 * D:]).then_inc(c_in, 16)
                sp.dma_start(fg[:], a["final_norm_g"].rearrange("(a n) -> a n", a=1).to_broadcast([P, D])).then_inc(c_in, 16)
                for t in range(TILES):
                    r = rows_of(t)
                    if t >= 4:
                        sp.wait_ge(y_ok, t - 3)
                    sp.dma_start(aa[0:r, t % 4, :], acc_d[ROW0 + t * P:ROW0 + t * P + r, :]).then_inc(t_in[t % 4], 16)
                    sp.dma_start(xx[0:r, t % 4, :], x2_d[t * P:t * P + r, :]).then_inc(t_in[t % 4], 16)

            @block.scalar
            def _(act):
                for t in range(TILES):
                    r = rows_of(t)
                    act.wait_ge(sum_ok, t + 1)
                    if t:
                        act.wait_ge(y_ok, t)
                    act.activation(sqj[0:r, :], aa[0:r, t % 4, :], ACT.Square, accum_out=st[0:r, 0:1]).then_inc(sq_ok, 1)
                    act.wait_ge(sq_ok, t + 1)
                    act.activation(st[0:r, 1:2], st[0:r, 0:1], ACT.Sqrt, scale=1.0 / D, bias=eps[0:r, 0:1]).then_inc(sd_ok, 1)

            @block.gpsimd
            def _(pool):
                for t in range(TILES):
                    r = rows_of(t)
                    pool.wait_ge(y_ok, t + 1)
                    pool.dma_start(y_p[t * P:(t + 1) * P, :] if t < TILES - 1 else y_s, yy[0:r, t % 2, :]).then_inc(out[t % 2], 16)
                for b in range(2):
                    pool.wait_ge(out[b], 16 * ((TILES + 1 - b) // 2))

            @block.vector
            def _(dve):
                s = Steps(dve, dve7)
                dve.wait_ge(c_in, 48)
                for t in range(TILES):
                    r = rows_of(t)
                    dve.wait_ge(t_in[t % 4], 32 * (t // 4 + 1))
                    acc = aa[0:r, t % 4, :]
                    s.link(dve.tensor_tensor(acc, acc, (g2 if t < TILES - 1 else g2s)[0:r, :], ALU.mult))
                    dve.tensor_tensor(acc, acc, xx[0:r, t % 4, :], ALU.add).then_inc(sum_ok, 1)
                    dve.wait_ge(sd_ok, t + 1)
                    s.link(dve.reciprocal(st[0:r, 2:3], st[0:r, 1:2]))
                    if t >= 2:
                        dve.wait_ge(out[t % 2], 16 * (t // 2))
                    dve.scalar_tensor_tensor(out=yy[0:r, t % 2, :], in0=acc, scalar=st[0:r, 2:3], in1=fg[0:r, :],
                                             op0=ALU.mult, op1=ALU.mult).then_inc(y_ok, 1)


_INS = ["x_prompt", "x_sample", "state_hgrn", "state_conv", "c_prompt", "c_sample", "w_ada", "b_ada", "norm_mix_g",
        "norm_ffn_g", "w_in", "lb_logits", "hgrn_norm_g", "conv_w", "conv_b", "w_out_hgrn", "w_out_conv", "w_o",
        "w_router", "router_bias", "w_exp_gate", "w_exp_up", "w_exp_down", "w_sh_gate", "w_sh_up", "w_sh_down",
        "final_norm_g"]
_OUTS = [("y_prompt", (1, T, D)), ("y_sample", (NS, 1, D)), ("hgrn_prompt", (1, 1, H, HK, HK)),
         ("conv_prompt", (1, 1, 2, W)), ("hgrn_sample", (1, NS, H, HK, HK)), ("conv_sample", (1, NS, 2, W))]


def kernel(**inputs):
    import concourse.bacc as bacc
    from concourse.bass_utils import run_bass_kernel_spmd

    nc = bacc.Bacc("TRN2", target_bir_lowering=False, num_devices=1)
    arrays, a, o = {}, {}, {}
    for name in _INS:
        arrays["in_" + name] = np.ascontiguousarray(inputs[name])
        a[name] = nc.dram_tensor("in_" + name, arrays["in_" + name].shape, F32, kind="ExternalInput").ap()
    for name, shape in _OUTS:
        o[name] = nc.dram_tensor("out_" + name, shape, F32, kind="ExternalOutput").ap()
    layer(nc, a, o)
    r = run_bass_kernel_spmd(nc, [arrays], core_ids=[0])
    return tuple(r.results[0]["out_" + name] for name, _ in _OUTS)
```

```python
from contextlib import ExitStack

import numpy as np

import concourse.bass as bass
from concourse import mybir

ALU = mybir.AluOpType
ACT = mybir.ActivationFunctionType
AX = mybir.AxisListType
F32 = mybir.dt.float32
F32R = mybir.dt.float32r
BF16 = mybir.dt.bfloat16
I32 = mybir.dt.int32
U32 = mybir.dt.uint32

P = 128
D = 1024
KD = D // P
T = 1024
NS = 8
TT = T + NS
TILES = T // P + 1
PIECE = TT // 3
PIECES = TT // PIECE
H = 4
HK = 128
W = 512
CH = W // P
CHUNK = 32
CPG = P // CHUNK
GROUPS = T // P
E = 64
EG = 8
FF = 256
TOPK, TOPG = 8, 4
SCALE = 2.5
EPS = 1e-6
ROW0 = 1
ROWS = ROW0 + TT + P
XW = D + E
ITEMS = 2 * E
SPAN = 8
AHEAD = 4
LISTS = 8
RING = 4
NEG = -1e30


def rows_of(t):
    return P if t < TILES - 1 else NS


class Steps:

    def __init__(self, eng, sem):
        self.eng, self.sem, self.n, self.shift = eng, sem, 0, 0

    def run(self, ins):
        ins.then_inc(self.sem, 1)
        self.n += 1

    def settle(self):
        self.eng.wait_ge(self.sem, self.shift + self.n)

    def link(self, ins):
        self.run(ins)
        self.settle()

    def enter(self, i, per):
        self.at, self.per = self.n, per
        self.shift = i * per

    def leave(self, times):
        assert self.n - self.at == self.per, (self.n - self.at, self.per)
        self.shift = 0
        self.n = self.at + self.per * times


def layer(nc, a, o):
    with ExitStack() as top:
        stage = top.enter_context(ExitStack())
        held = []

        def sem(name):
            held.append(stage.enter_context(nc.semaphore(name)))
            return held[-1]

        def next_stage():
            with nc.Block() as block:
                @block.gpsimd
                def _(pool):
                    for s in held:
                        pool.sem_clear(s)
            held.clear()
            stage.close()

        def sb(name, shape, dt=F32, ctx=top, side=None):
            return ctx.enter_context(nc.sbuf_tensor(name, shape, dt, side=side))

        banks = [top.enter_context(nc.psum_tensor(f"bank{i}", [P, 512], F32)) for i in range(8)]

        mod_d = nc.dram_tensor("mod_d", [NS + 1, 6 * D], F32).ap()
        gates_d = nc.dram_tensor("gates_d", [2 * KD, P, TT], F32).ap()
        x2_d = nc.dram_tensor("x2_d", [TT, D], F32).ap()
        xe_d = nc.dram_tensor("xe_d", [ROWS, XW], F32).ap()
        acc_d = nc.dram_tensor("acc_d", [ROWS, D], F32).ap()

        ident = sb("ident", [P, P])
        eps = sb("eps", [P, 1])
        at = -(-nc.sbuf_base // 32) * 32
        hT = sb("hT", [P, KD, TT])
        hT_hi = nc.alloc_sbuf_tensor_at("hT_hi", [P, KD, TT], F32R, offset=at)
        assert nc.sbuf_base == at + KD * TT * 4

        x_p = a["x_prompt"].rearrange("b t d -> (b t) d")
        x_s = a["x_sample"].rearrange("b t d -> (b t) d")

        def x_rows(t):
            return x_p[t * P:(t + 1) * P, :] if t < TILES - 1 else x_s

        w_in = a["w_in"].rearrange("l (k p) n -> p (l k) n", p=P)

        NPAR = KD + 2 * CH + H + 3 * CH + CH
        par = sb("par", [P, NPAR])
        split = top.enter_context(ExitStack())
        hT_lo = sb("hT_lo", [P, KD, TT], F32R, split, "right")
        with ExitStack() as c1:
            par_rows = sb("par_rows", [NPAR, P], ctx=c1)
            c_rows = sb("c_rows", [NS + 1, D], ctx=c1)
            cT = sb("cT", [P, KD, NS + 1], ctx=c1)
            wada = sb("wada", [P, 3, KD, 512], ctx=c1)
            mod = sb("mod", [NS + 1, 6 * D], ctx=c1)
            modT = sb("modT", [P, 2 * KD, NS + 1], ctx=c1)
            xn = sb("xn", [P, TILES, D], ctx=c1)
            high = sb("high", [P, 2, TT], F32R, c1)
            ssq = sb("ssq", [P, TILES], ctx=c1)
            rstd = sb("rstd", [P, TILES], ctx=c1)
            par_in, c_in, b_in, x_in = sem("par_in"), sem("c_in"), sem("b_in"), sem("x_in")
            ada_in = [sem(f"ada_in{i}") for i in range(3)]
            ident_ok, par_T, par_ok, c_ok, cT_ok, cT_cp = (
                sem(n) for n in ("ident_ok", "par_T", "par_ok", "c_ok", "cT_ok", "cT_cp"))
            mod_ps, mod_ok, modT_ps, modT_ok, mod_out = (
                sem(n) for n in ("mod_ps", "mod_ok", "modT_ps", "modT_ok", "mod_out"))
            ssq_ok, sd_ok, xn_ok, xT_ps, hT_ok, hT_s_ok = (
                sem(n) for n in ("ssq_ok", "sd_ok", "xn_ok", "xT_ps", "hT_ok", "hT_s_ok"))
            dve1, pool1 = sem("dve1"), sem("pool1")
            hT_n_ok, high_ok, lo_ok, hi_ok = sem("hT_n_ok"), sem("high_ok"), sem("lo_ok"), sem("hi_ok")
            NADA = 6 * D // 512
            ada_v = a["w_ada"].rearrange("l (k p) n -> p (l k) n", p=P)
            O_G, O_LB, O_HG, O_CW, O_CB = 0, KD, KD + 2 * CH, KD + 2 * CH + H, KD + 2 * CH + H + 3 * CH
            with nc.Block() as block:
                @block.sync
                def _(sp):
                    for at, src in ((O_G, a["norm_mix_g"].rearrange("l (k p) -> (l k) p", p=P)),
                                    (O_LB, a["lb_logits"].rearrange("l (k p) -> (l k) p", p=P)),
                                    (O_HG, a["hgrn_norm_g"].rearrange("l h p -> (l h) p")),
                                    (O_CW, a["conv_w"].rearrange("l j (k p) -> (l j k) p", p=P)),
                                    (O_CB, a["conv_b"].rearrange("l (k p) -> (l k) p", p=P))):
                        sp.dma_start(par_rows[at:at + src.shape[0], :], src).then_inc(par_in, 16)
                    sp.dma_start(c_rows[0:NS, :], a["c_sample"]).then_inc(c_in, 16)
                    sp.dma_start(c_rows[NS:NS + 1, :], a["c_prompt"]).then_inc(c_in, 16)
                    sp.dma_start(mod[:], a["b_ada"].to_broadcast([NS + 1, 6 * D])).then_inc(b_in, 16)
                    for n in range(NADA):
                        if n >= 3:
                            sp.wait_ge(mod_ps, n - 2)
                        sp.dma_start(wada[:, n % 3], ada_v[:, :, n * 512:(n + 1) * 512]).then_inc(ada_in[n % 3], 16)
                    sp.wait_ge(mod_ok, NADA)
                    sp.dma_start(mod_d, mod[:]).then_inc(mod_out, 16)
                    sp.wait_ge(mod_out, 16)

                @block.gpsimd
                def _(pool):
                    pool.memset(ident[:], 0.0).then_inc(pool1, 1)
                    pool.wait_ge(pool1, 1)
                    pool.affine_select(out=ident[:], in_=ident[:], compare_op=ALU.not_equal, fill=1.0, base=0,
                                       pattern=[[-1, P]], channel_multiplier=1).then_inc(ident_ok, 1)
                    pool.memset(eps[:], EPS).then_inc(ident_ok, 1)

                @block.scalar
                def _(act):
                    for t in range(TILES):
                        act.dma_start(xn[0:rows_of(t), t, :], x_rows(t)).then_inc(x_in, 16)
                    act.wait_ge(c_in, 32)
                    act.activation(c_rows[:], c_rows[:], ACT.Silu).then_inc(c_ok, 1)
                    act.wait_ge(x_in, 16 * TILES)
                    for t in range(TILES):
                        if t:
                            act.wait_ge(ssq_ok, t)
                        act.activation(high[0:rows_of(t), 0, 0:D], xn[0:rows_of(t), t, :], ACT.Square,
                                       accum_out=ssq[0:rows_of(t), t:t + 1]).then_inc(ssq_ok, 1)
                    act.wait_ge(ident_ok, 2)
                    act.wait_ge(ssq_ok, TILES)
                    act.activation(rstd[:, 0:TILES - 1], ssq[:, 0:TILES - 1], ACT.Sqrt, scale=1.0 / D,
                                   bias=eps[:, 0:1]).then_inc(sd_ok, 1)
                    act.activation(rstd[0:NS, TILES - 1:], ssq[0:NS, TILES - 1:], ACT.Sqrt, scale=1.0 / D,
                                   bias=eps[0:NS, 0:1]).then_inc(sd_ok, 1)
                    act.wait_ge(modT_ok, 1)
                    for k in range(KD):
                        act.wait_ge(xT_ps, 2 * k + 1)
                        act.activation(hT[:, k, 0:512], banks[2 + (2 * k) % 4][:], ACT.Identity,
                                       scale=modT[:, KD + k, NS:NS + 1], bias=modT[:, k, NS:NS + 1]).then_inc(hT_ok, 1)

                    def high_part(k):
                        act.wait_ge(lo_ok, k + 1)
                        act.activation(hT_hi[:, k, :], high[:, k % 2, :], ACT.Copy).then_inc(hi_ok, 1)

                    act.wait_ge(hT_n_ok, 1)
                    for k in range(KD):
                        if k >= 2:
                            act.wait_ge(hi_ok, k - 1)
                        else:
                            act.wait_ge(hT_ok, KD)
                        act.activation(high[:, k % 2, :], hT[:, k, :], ACT.Copy).then_inc(high_ok, 1)
                        if k:
                            high_part(k - 1)
                    high_part(KD - 1)

                @block.tensor
                def _(pe):
                    pe.wait_ge(ident_ok, 1)
                    pe.wait_ge(par_in, 16 * 5)
                    pe.transpose(banks[0][:, 0:NPAR], par_rows[:], ident[0:NPAR, 0:NPAR]).then_inc(par_T, 1)
                    pe.wait_ge(c_ok, 1)
                    for k in range(KD):
                        last = pe.transpose(banks[1][:, k * (NS + 1):(k + 1) * (NS + 1)], c_rows[:, k * P:(k + 1) * P],
                                            ident[0:NS + 1, 0:NS + 1])
                    last.then_inc(cT_ok, 1)
                    pe.wait_ge(cT_cp, 1)

                    def cond(n):
                        pe.wait_ge(ada_in[n % 3], 16 * (n // 3 + 1))
                        if n >= 2:
                            pe.wait_ge(mod_ok, n - 1)
                        for k in range(KD):
                            last = pe.matmul(banks[n % 2][0:NS + 1, :], cT[:, k, :], wada[:, n % 3, k, :],
                                             start=(k == 0), stop=(k == KD - 1))
                        last.then_inc(mod_ps, 1)

                    for n in range(4):
                        cond(n)
                    pe.wait_ge(mod_ok, 4)
                    for k in range(2 * KD):
                        last = pe.transpose(banks[2][:, k * (NS + 1):(k + 1) * (NS + 1)], mod[:, k * P:(k + 1) * P],
                                            ident[0:NS + 1, 0:NS + 1])
                    last.then_inc(modT_ps, 1)
                    pe.wait_ge(modT_ok, 1)
                    pe.wait_ge(xn_ok, TILES)
                    for k in range(KD):
                        for half in range(2):
                            n = 2 * k + half
                            if n >= 4:
                                pe.wait_ge((hT_ok, hT_s_ok)[half], k - 1)
                            for j in range(4):
                                t = 4 * half + j
                                last = pe.transpose(banks[2 + n % 4][:, j * P:(j + 1) * P], xn[:, t, k * P:(k + 1) * P],
                                                    ident[:])
                            last.then_inc(xT_ps, 1)
                    for k in range(KD):
                        last = pe.transpose(banks[6][:, k * NS:(k + 1) * NS], xn[0:NS, TILES - 1, k * P:(k + 1) * P],
                                            ident[0:NS, 0:NS])
                    last.then_inc(xT_ps, 1)
                    for n in range(4, NADA):
                        cond(n)

                @block.vector
                def _(dve):
                    s = Steps(dve, dve1)
                    dve.wait_ge(par_T, 1)
                    s.link(dve.tensor_copy(par[:], banks[0][:, 0:NPAR]))
                    dve.wait_ge(cT_ok, 1)
                    dve.tensor_copy(cT[:].rearrange("p k c -> p (k c)"), banks[1][:, 0:KD * (NS + 1)]).then_inc(cT_cp, 1)
                    dve.wait_ge(sd_ok, 2)
                    s.run(dve.reciprocal(rstd[:, 0:TILES - 1], rstd[:, 0:TILES - 1]))
                    s.link(dve.reciprocal(rstd[0:NS, TILES - 1:], rstd[0:NS, TILES - 1:]))
                    for t in range(TILES):
                        r = rows_of(t)
                        dve.tensor_scalar(xn[0:r, t, :], xn[0:r, t, :], rstd[0:r, t:t + 1], None,
                                          ALU.mult).then_inc(xn_ok, 1)

                    def cond(n):
                        dve.wait_ge(mod_ps, n + 1)
                        dve.tensor_tensor(mod[:, n * 512:(n + 1) * 512], banks[n % 2][0:NS + 1, :],
                                          mod[:, n * 512:(n + 1) * 512], ALU.add).then_inc(mod_ok, 1)

                    dve.wait_ge(b_in, 16)
                    for n in range(4):
                        cond(n)
                    dve.wait_ge(modT_ps, 1)
                    s.run(dve.tensor_copy(modT[:, 0:KD].rearrange("p k c -> p (k c)"), banks[2][:, 0:KD * (NS + 1)]))
                    m = KD * (NS + 1)
                    s.link(dve.tensor_scalar(modT[:, KD:].rearrange("p k c -> p (k c)"), banks[2][:, m:2 * m], 1.0, None,
                                             ALU.add))
                    dve.tensor_tensor(modT[:, KD:], modT[:, KD:],
                                      par[:, O_G:O_G + KD].unsqueeze(2).to_broadcast([P, KD, NS + 1]),
                                      ALU.mult).then_inc(modT_ok, 1)
                    dve.wait_ge(modT_ok, 1)
                    for k in range(KD):
                        dve.wait_ge(xT_ps, 2 * k + 2)
                        dve.tensor_scalar(hT[:, k, 512:T], banks[2 + (2 * k + 1) % 4][:], modT[:, KD + k, NS:NS + 1],
                                          modT[:, k, NS:NS + 1], ALU.mult, ALU.add).then_inc(hT_s_ok, 1)
                    dve.wait_ge(xT_ps, 2 * KD + 1)
                    s.link(dve.tensor_tensor(hT[:, :, T:], banks[6][:, 0:KD * NS].rearrange("p (k c) -> p k c", c=NS),
                                             modT[:, KD:, 0:NS], ALU.mult))
                    dve.tensor_tensor(hT[:, :, T:], hT[:, :, T:], modT[:, 0:KD, 0:NS], ALU.add).then_inc(hT_n_ok, 1)
                    for k in range(KD):
                        dve.wait_ge(high_ok, k + 1)
                        dve.tensor_tensor(hT_lo[:, k, :], hT[:, k, :], high[:, k % 2, :], ALU.subtract).then_inc(lo_ok, 1)
                        cond(4 + k)

        with ExitStack() as c2:
            qT = sb("qT", [P, CH, TT], ctx=c2)
            gT = sb("gT", [P, CH, TT], ctx=c2)
            bT = sb("bT", [P, CH, TT], ctx=c2)
            with ExitStack() as c3:
                fT = sb("fT", [P, CH, TT], ctx=c3)
                cvT = sb("cvT", [P, CH, TT], ctx=c3)
                vv = sb("vv", [P, TILES, W], ctx=c3)
                with ExitStack() as c4:
                    next_stage()
                    project_in(nc, a, c4, sb, sem, banks, w_in, hT, hT_hi, hT_lo, qT, fT, gT, bT, cvT, vv)
                split.close()
                next_stage()
                token_mixers(nc, a, o, sb, sem, banks, par, ident, eps, w_in, gates_d, hT, qT, fT, gT, bT, cvT, vv,
                             (O_LB, O_HG, O_CW, O_CB))
            mT = sb("mT", [P, KD, TT], ctx=c2)
            next_stage()
            merge(nc, a, sb, sem, banks, gates_d, qT, bT, mT)
            next_stage()
            output_and_norm(nc, a, sb, sem, banks, ident, eps, mod_d, x2_d, xe_d, x_rows, mT, hT)
        with ExitStack() as c5:
            wexp = sb("wexp", [P, RING, KD + 4, 512], ctx=c5)
            posm = sb("posm", [P, E + 1, TILES], ctx=c5)
            table = sb("table", [1, ITEMS + AHEAD, 2], I32, ctx=c5)
            total = sb("total", [1, 1], I32, ctx=c5)
            tok = sb("tok", [P, TILES, 2], BF16, ctx=c5)
            idle = sb("idle", [P, 1], ctx=c5)
            iota = sb("iota", [P, TILES * P], ctx=c5)
            next_stage()
            slot_in = [top.enter_context(nc.semaphore(f"slot_in{i}")) for i in range(RING)]
            routing(nc, a, sb, sem, banks, hT, xe_d, acc_d, posm, table, total, tok, idle, iota, wexp, slot_in)
            next_stage()
            experts(nc, a, sb, sem, banks, ident, xe_d, acc_d, posm, table, total, tok, idle, iota, wexp, slot_in)
        next_stage()
        final(nc, a, o, sb, sem, eps, mod_d, x2_d, acc_d)


def project_in(nc, a, ctx, sb, sem, banks, w_in, hT, hT_hi, hT_lo, qT, fT, gT, bT, cvT, vv):
    raw = sb("w_raw", [P, KD, P], ctx=ctx)
    w_hi = sb("w_hi", [P, CH, KD, P], F32R, ctx)
    w_lo = sb("w_lo", [P, CH, KD, P], F32R, ctx)
    raw_in, hi_ok, w_ready, w_used = (sem(n) for n in "raw_in w_hi_ok w_ready w_used".split())
    passed = sem("w_passed")
    ps_full, ps_read, whole = sem("proj_full"), sem("proj_read"), sem("whole")
    PER = CH * PIECES
    VPER = 2 * TILES
    NB = 6
    PASSES = 7
    with nc.Block() as block:
        @block.sync
        def _(sp):
            sp.dma_start(raw[:], w_in[:, :, 0:P]).then_inc(raw_in, 16)
            with sp.Fori(1, PASSES * CH) as u:
                sp.wait_ge(w_ready, u)
                sp.dma_start(raw[:], w_in[:, :, bass.ds(u * P, P)]).then_inc(raw_in, 16)

        @block.gpsimd
        def _(pool):
            with pool.Fori(0, PASSES) as i:
                for c in range(CH):
                    pool.wait_ge(raw_in, i * (16 * CH) + 16 * c + 16)
                    pool.wait_ge(w_used, i * CH + c + 1)
                    pool.sem_inc(passed, 1)
                    pool.tensor_copy(w_hi[:, c], raw[:]).then_inc(hi_ok, 1)

        @block.tensor
        def _(pe):
            pe.sem_inc(w_used, CH)

            def terms(bank, stat_hi, stat_lo, mov_hi, mov_lo):
                for k in range(KD):
                    for x, (stat, mov) in enumerate(((stat_hi, mov_hi), (stat_hi, mov_lo), (stat_lo, mov_hi))):
                        last = pe.matmul(bank, stat(k), mov(k), start=(k == 0 and x == 0), stop=(k == KD - 1 and x == 2))
                return last

            def used(c, n=1):
                pe.matmul(banks[7][:, 0:2], w_hi[:, c, 0, 0:P], w_hi[:, c, 0, 0:2], start=True, stop=True).then_inc(w_used, n)

            def tensor_pass(i, first):
                for c in range(CH):
                    pe.wait_ge(w_ready, i * CH + c + 1)
                    for n in range(PIECES):
                        r = c * PIECES + n
                        toks = slice(n * PIECE, (n + 1) * PIECE)
                        pe.wait_ge(ps_read, first + r + 1)
                        terms(banks[r % NB][:, 0:PIECE], lambda k: w_hi[:, c, k, :], lambda k: w_lo[:, c, k, :],
                              lambda k: hT_hi[:, k, toks], lambda k: hT_lo[:, k, toks]).then_inc(ps_full, 1)
                    used(c)

            with pe.Fori(0, 2) as i:
                tensor_pass(i, i * PER)
            for j in range(2):
                pe.wait_ge(w_ready, 2 * CH + 2 * j + 2)
                for t in range(TILES):
                    r = j * TILES + t
                    pe.wait_ge(ps_read, 2 * PER + r + 1)
                    m = rows_of(t)
                    toks = slice(t * P, t * P + m)
                    terms(banks[r % NB][0:m, 0:2 * P].rearrange("p (c n) -> p c n", n=P),
                          lambda k: hT_hi[:, k, toks], lambda k: hT_lo[:, k, toks],
                          lambda k: w_hi[:, 2 * j:2 * j + 2, k, :],
                          lambda k: w_lo[:, 2 * j:2 * j + 2, k, :]).then_inc(ps_full, 1)
                used(2 * j + 1, 2)
            with pe.Fori(3, PASSES) as i:
                tensor_pass(i, (i - 1) * PER + VPER)

        @block.scalar
        def _(act):
            act.sem_inc(ps_read, NB)

            def take(dst, func, first):
                for c in range(CH):
                    for n in range(PIECES):
                        r = c * PIECES + n
                        act.wait_ge(ps_full, first + r + 1)
                        act.activation(dst[:, c, n * PIECE:(n + 1) * PIECE], banks[r % NB][:, 0:PIECE],
                                       func).then_inc(ps_read, 1)

            take(qT, ACT.Silu, 0)
            take(fT, ACT.Sigmoid, PER)
            for r in range(VPER):
                act.wait_ge(ps_full, 2 * PER + r + 1)
                j, t = divmod(r, TILES)
                m = rows_of(t)
                act.activation(vv[0:m, t, j * 2 * P:(j + 1) * 2 * P], banks[r % NB][0:m, 0:2 * P],
                               ACT.Copy).then_inc(ps_read, 1)
            take(gT, ACT.Silu, 2 * PER + VPER)
            take(bT, ACT.Copy, 3 * PER + VPER)
            take(cvT, ACT.Copy, 4 * PER + VPER)

        @block.vector
        def _(dve):
            with dve.Fori(0, PASSES) as i:
                for c in range(CH):
                    dve.wait_ge(hi_ok, i * CH + c + 1)
                    dve.tensor_tensor(w_lo[:, c], raw[:], w_hi[:, c], ALU.subtract).then_inc(w_ready, 1)
            for r in range(PER):
                c, n = divmod(r, PIECES)
                dve.wait_ge(ps_full, 5 * PER + VPER + r + 1)
                dve.wait_ge(ps_read, 5 * PER + VPER + NB + r)
                at = cvT[:, c, n * PIECE:(n + 1) * PIECE]
                dve.tensor_tensor(at, at, banks[r % NB][:, 0:PIECE], ALU.mult).then_inc(ps_read, 1)
            for k in range(KD):
                dve.tensor_tensor(hT[:, k, :], hT_hi[:, k, :], hT_lo[:, k, :], ALU.add).then_inc(whole, 1)


def token_mixers(nc, a, o, sb, sem, banks, par, ident, eps, w_in, gates_d, hT, qT, fT, gT, bT, cvT, vv, offsets):
    O_LB, O_HG, O_CW, O_CB = offsets
    GA = 7 * W
    with ExitStack() as ctx:
        onesm = sb("onesm", [P, P], ctx=ctx)
        wg = [sb(f"wg{j}", [P, KD, P], ctx=ctx) for j in range(2)]
        gst = sb("gst", [P, PIECES, PIECE], ctx=ctx)
        wg_in = [sem("wg_in0"), sem("wg_in1")]
        gate_ps, gate_read, gate_free = sem("gate_ps"), sem("gate_read"), sem("gate_free")
        gate_out = [sem(f"gate_out{n}") for n in range(PIECES)]

        def gate_product(pe, tile, j, n):
            if n == 0:
                pe.wait_ge(wg_in[j], 16 * (tile // 2) + 16)
            pe.wait_ge(gate_read, tile * PIECES + n + 1)
            for k in range(KD):
                last = pe.matmul(banks[7][:, 0:PIECE], wg[j][:, k, :], hT[:, k, n * PIECE:(n + 1) * PIECE],
                                 start=(k == 0), stop=(k == KD - 1))
            last.then_inc(gate_ps, 1)

        def load_gate(sp, tile, j):
            sp.dma_start(wg[j][:], w_in[:, :, bass.ds(tile * P + GA, P)]).then_inc(wg_in[j], 16)

        def take_gate(act, tile, n):
            act.wait_ge(gate_ps, tile * PIECES + n + 1)
            act.wait_ge(gate_free, tile * PIECES + n + 1)
            act.activation(gst[:, n, :], banks[7][:, 0:PIECE], ACT.Copy).then_inc(gate_read, 1)

        def store_gate(pool, tile):
            for n in range(PIECES):
                pool.wait_ge(gate_read, tile * PIECES + n + 2)
                pool.dma_start(gates_d[bass.ds(tile, 1), :, n * PIECE:(n + 1) * PIECE].rearrange("a p t -> p (a t)"),
                               gst[:, n, :]).then_inc(gate_out[n], 16)
            for n in range(PIECES):
                pool.wait_ge(gate_out[n], tile * 16 + 16)
                pool.sem_inc(gate_free, 1)

        chunks = ExitStack()
        tile = lambda name, shape, dt=F32: sb(name, shape, dt, chunks)
        lb = tile("lb", [P, H])
        omlb = tile("omlb", [P, H])
        lbt = tile("lbt", [P, 4, H])
        reset = tile("reset", [P, W])
        causal = tile("causal", [P, H, P], I32)
        lnf = tile("lnf", [P, W])
        cum = tile("cum", [P, W])
        ex = tile("ex", [P, 2, W])
        exi = tile("exi", [P, W])
        exe = tile("exe", [P, W])
        rest = lnf
        kk = tile("kk", [P, W])
        qin = tile("qin", [P, 2, W])
        kin = tile("kin", [P, W])
        kend = tile("kend", [P, 2, W])
        kendR = tile("kendR", [P, W])
        vst = tile("vst", [P, W])
        vblk = tile("vblk", [P, H, CPG, HK])
        attm = tile("attm", [P, 2, W])
        S = tile("S", [P, CPG + 1, W])

        names = ("mk_lb mk_ln mk_cum mk_exp mk_rest mk_exe mk_q mk_k mk_kT mk_kR mk_att mk_am mk_v mk_U mk_S "
                 "mk_o mk_oc mk_f mk_const").split()
        (lb_ok, ln_ok, cum_ok, exp_ok, rest_ok, exe_ok, qk_ok, kend_ok, kT_ps, kR_ok, att_ps, am_ok, v_ok,
         U_ps, S_ok, o_ps, o_ok, f_ok, const_ok) = (sem(n) for n in names)
        dve2, pool2 = sem("dve2"), sem("pool2")
        st_out = sem("st_out")
        passed = sem("mk_passed")
        att_b, kT_b, o_b = banks[4], banks[5], banks[6]
        PAIRS = GROUPS // 2

        def grp(x, g):
            return x[:, :, bass.ds(g * P, P)]

        def h3(x):
            return x.rearrange("p (h t) -> p h t", h=H)

        def slot(b, j):
            return (CPG * b + j) % (2 * CPG) if j in (0, CPG) else j

        def groups(eng, prepare, finish, enter=None, leave=None):
            prepare(0, 0)
            with eng.Fori(0, PAIRS - 1) as i:
                if enter:
                    enter(i)
                for b in range(2):
                    finish(2 * i + b, b, lambda *amid: prepare(2 * i + b + 1, 1 - b, *amid))
            if leave:
                leave(PAIRS - 1)
            finish(GROUPS - 2, 0, lambda *amid: prepare(GROUPS - 1, 1, *amid))
            finish(GROUPS - 1, 1, lambda *amid: [step() for step in amid])

        with nc.Block() as block:
            @block.gpsimd
            def _(pool):
                pool.memset(reset[:], 1.0).then_inc(pool2, 1)
                pool.memset(onesm[:], 1.0).then_inc(const_ok, 1)
                pool.memset(causal[:], 1).then_inc(pool2, 1)
                pool.wait_ge(pool2, 2)
                pool.memset(reset[:].rearrange("p (c t) -> p c t", t=CHUNK)[:, :, 0:1], 0.0).then_inc(const_ok, 1)
                pool.affine_select(out=causal[:], in_=causal[:], compare_op=ALU.is_ge, fill=0.0, base=0,
                                   pattern=[[0, H], [1, P]], channel_multiplier=-1).then_inc(pool2, 1)
                for c in range(1, CPG):
                    pool.wait_ge(pool2, 2 + c)
                    v = causal[:, :, c * CHUNK:(c + 1) * CHUNK]
                    pool.affine_select(out=v, in_=v, compare_op=ALU.is_ge, fill=0.0, base=-c * CHUNK,
                                       pattern=[[0, H], [0, CHUNK]], channel_multiplier=1).then_inc(pool2, 1)
                pool.wait_ge(pool2, 2 + CPG)
                pool.memset(attm[:], 0.0).then_inc(const_ok, 1)
                pool.memset(S[:, 0, :], 0.0).then_inc(const_ok, 1)
                pool.memset(vblk[:], 0.0).then_inc(const_ok, 1)
                pool.sem_inc(gate_read, 1)
                pool.sem_inc(gate_free, PIECES)
                with pool.Fori(0, GROUPS) as g:
                    store_gate(pool, g)

            @block.scalar
            def _(act):
                act.wait_ge(lb_ok, 1)
                act.activation(lbt[:, 0:2, :], lbt[:, 0:2, :], ACT.Exp).then_inc(lb_ok, 1)
                act.wait_ge(f_ok, 1)
                act.wait_ge(const_ok, 5)

                def prepare(g, b, between=None):
                    act.activation(h3(lnf[:]), grp(fT, g), ACT.Ln).then_inc(ln_ok, 1)
                    act.wait_ge(cum_ok, g + 1)
                    act.activation(ex[:, b], cum[:], ACT.Exp).then_inc(exp_ok, 1)
                    act.activation(exi[:], cum[:], ACT.Exp, scale=-1.0).then_inc(exp_ok, 1)
                    if between:
                        between()
                    act.wait_ge(rest_ok, g + 1)
                    act.activation(exe[:], rest[:], ACT.Exp).then_inc(exe_ok, 1)

                def finish(g, b, ahead):
                    for j in range(CPG):
                        rows = slice(j * CHUNK, (j + 1) * CHUNK)
                        act.activation(vblk[rows, :, j, :], vv[rows, bass.ds(g, 1), :].rearrange(
                            "p a (h v) -> p (a h) v", h=H), ACT.Copy).then_inc(v_ok, 1)
                    act.wait_ge(kT_ps, g + 1)
                    act.activation(kendR[:], kT_b[:], ACT.Copy).then_inc(kR_ok, 1)
                    act.activation(vst[:], vv[:, bass.ds(g, 1), :].rearrange("p a n -> p (a n)"),
                                   ACT.Copy).then_inc(v_ok, 1)
                    ahead(lambda: take_gate(act, g, 0))
                    take_gate(act, g, 1)
                    take_gate(act, g, 2)
                    act.wait_ge(o_ps, g + 2)
                    act.activation(grp(qT, g), h3(o_b[:]), ACT.Copy).then_inc(o_ok, 1)

                groups(act, prepare, finish)

            @block.vector
            def _(dve):
                s = Steps(dve, dve2)
                l0, l1 = par[:, O_LB:O_LB + H], par[:, O_LB + H:O_LB + 2 * H]
                s.link(dve.tensor_tensor(lbt[:, 2, :], l0, l1, ALU.max))
                s.run(dve.tensor_tensor(lbt[:, 0, :], l0, lbt[:, 2, :], ALU.subtract))
                s.run(dve.tensor_tensor(lbt[:, 1, :], l1, lbt[:, 2, :], ALU.subtract))
                s.settle()
                dve.sem_inc(lb_ok, 1)
                dve.wait_ge(lb_ok, 2)
                s.link(dve.tensor_tensor(lbt[:, 2, :], lbt[:, 0, :], lbt[:, 1, :], ALU.add))
                s.link(dve.reciprocal(lbt[:, 3, :], lbt[:, 2, :]))
                s.link(dve.tensor_tensor(lb[:], lbt[:, 0, :], lbt[:, 3, :], ALU.mult))
                s.link(dve.tensor_scalar(omlb[:], lb[:], -1.0, 1.0, ALU.mult, ALU.add))
                for h in range(H):
                    s.run(dve.tensor_scalar(fT[:, h, :], fT[:, h, :], omlb[:, h:h + 1], lb[:, h:h + 1], ALU.mult, ALU.add))
                s.settle()
                dve.sem_inc(f_ok, 1)
                dve.wait_ge(const_ok, 5)

                def prepare(g, b):
                    dve.wait_ge(ln_ok, g + 1)
                    dve.tensor_tensor_scan(cum[:], reset[:], lnf[:], 0.0, ALU.mult, ALU.add).then_inc(cum_ok, 1)
                    s.run(dve.tensor_scalar(h3(kk[:]), grp(fT, g), -1.0, 1.0, ALU.mult, ALU.add))
                    dve.wait_ge(cum_ok, g + 1)
                    c3 = cum[:].rearrange("p (c t) -> p c t", t=CHUNK)
                    dve.tensor_tensor(rest[:].rearrange("p (c t) -> p c t", t=CHUNK),
                                      c3[:, :, CHUNK - 1:CHUNK].to_broadcast([P, H * CPG, CHUNK]), c3,
                                      ALU.subtract).then_inc(rest_ok, 1)
                    dve.wait_ge(exp_ok, 2 * g + 2)
                    dve.wait_ge(o_ps, g)
                    s.settle()
                    s.run(dve.tensor_tensor(h3(qin[:, b]), grp(qT, g), h3(ex[:, b]), ALU.mult))
                    s.run(dve.tensor_tensor(kin[:], kk[:], exi[:], ALU.mult))
                    s.settle()
                    dve.sem_inc(qk_ok, 1)
                    dve.wait_ge(exe_ok, g + 1)
                    dve.tensor_tensor(kend[:, b], kk[:], exe[:], ALU.mult).then_inc(kend_ok, 1)
                    dve.wait_ge(kend_ok, g + 1)

                def finish(g, b, ahead):
                    dve.wait_ge(att_ps, g + 1)
                    dve.sem_inc(passed, 1)
                    dve.copy_predicated(attm[:, b], causal[:].rearrange("p h t -> p (h t)"),
                                        att_b[:]).then_inc(am_ok, 1)
                    ahead()
                    dve.wait_ge(U_ps, g + 1)
                    for j in range(CPG):
                        for h in range(H):
                            at = slice(h * HK, (h + 1) * HK)
                            last = h * P + j * CHUNK + CHUNK - 1
                            s.run(dve.scalar_tensor_tensor(
                                out=S[:, slot(b, j + 1), at], in0=S[:, slot(b, j), at],
                                scalar=ex[:, b, last:last + 1], in1=banks[h][:, j * HK:(j + 1) * HK],
                                op0=ALU.mult, op1=ALU.add))
                        s.settle()
                        if j >= CPG - 2:
                            dve.sem_inc(S_ok, 1)

                groups(dve, prepare, finish, lambda i: s.enter(i, 2 * (3 + CPG * H)), s.leave)

            @block.tensor
            def _(pe):
                for ahead_by_one in (am_ok, kR_ok, S_ok, o_ok, o_ps):
                    pe.sem_inc(ahead_by_one, 1)

                def prepare(g, b):
                    pe.wait_ge(qk_ok, g + 1)
                    pe.wait_ge(am_ok, g + 1)
                    for h in range(H):
                        at = slice(h * HK, (h + 1) * HK)
                        last = pe.matmul(att_b[:, at], kin[:, at], qin[:, b, at], start=True, stop=True)
                    last.then_inc(att_ps, 1)

                def finish(g, b, ahead):
                    pe.wait_ge(kend_ok, g + 1)
                    pe.wait_ge(kR_ok, g + 1)
                    for h in range(H):
                        at = slice(h * HK, (h + 1) * HK)
                        last = pe.transpose(kT_b[:, at], kend[:, b, at], ident[:])
                    last.then_inc(kT_ps, 1)
                    gate_product(pe, g, b, 0)
                    pe.wait_ge(kR_ok, g + 2)
                    pe.wait_ge(v_ok, (CPG + 1) * g + CPG)
                    pe.wait_ge(S_ok, 2 * g + 1)
                    for h in range(H):
                        last = pe.matmul(banks[h][:], kendR[:, h * HK:(h + 1) * HK],
                                         vblk[:, h].rearrange("p j v -> p (j v)"), start=True, stop=True)
                    last.then_inc(U_ps, 1)
                    gate_product(pe, g, b, 1)
                    ahead()
                    gate_product(pe, g, b, 2)
                    pe.wait_ge(am_ok, g + 2)
                    pe.wait_ge(v_ok, (CPG + 1) * g + CPG + 1)
                    pe.wait_ge(S_ok, 2 * g + 2)
                    pe.wait_ge(o_ok, g + 1)
                    for h in range(H):
                        at = slice(h * HK, (h + 1) * HK)
                        pe.matmul(o_b[:, at], vst[:, at], attm[:, b, at], start=(h == 0), stop=False,
                                  skip_group_check=True)
                    for h in range(H):
                        for j in range(CPG):
                            cols = slice(h * P + j * CHUNK, h * P + (j + 1) * CHUNK)
                            last = pe.matmul(o_b[:, cols], S[:, slot(b, j), h * HK:(h + 1) * HK], qin[:, b, cols],
                                             start=False, stop=(h == H - 1 and j == CPG - 1), skip_group_check=True)
                    last.then_inc(o_ps, 1)

                groups(pe, prepare, finish)

            @block.sync
            def _(sp):
                for j in range(2):
                    load_gate(sp, j, j)
                with sp.Fori(1, PAIRS + 1) as i:
                    for j in range(2):
                        sp.wait_ge(gate_ps, (2 * i + j - 1) * PIECES)
                        load_gate(sp, 2 * i + j, j)
                sp.wait_ge(S_ok, 2 * GROUPS + 1)
                sp.dma_start(o["hgrn_prompt"].rearrange("l b h d v -> d (l b h) v"),
                             S[:, 0, :].rearrange("p (h v) -> p h v", h=H)).then_inc(st_out, 16)
                sp.wait_ge(st_out, 16)

        chunks.close()
        tile = lambda name, shape, dt=F32: sb(name, shape, dt, ctx)
        conv = tile("conv", [P, T])
        sin = tile("sin", [P, 2, W])
        snew = tile("snew", [P, 2, W])
        stmp = tile("stmp", [P, W])
        sel = tile("sel", [NS, NS, P])
        ks = tile("ks", [P, H, NS])
        cst = tile("cst", [NS * 2, W])
        cstT = tile("cstT", [P, CH, NS * 2])
        cso = tile("cso", [NS + 2, W])
        names = "sm_in0 sm_in1 sm_out0 sm_out1 sm_sel sm_sel0 sm_v sm_new sm_k sm_o sm_oc sm_cs sm_cT sm_cTc sm_u sm_uo sm_co".split()
        (in0, in1, out0, out1, sel_ok, sel0, vb_ps, new_ok, ks_ok, os_ps, os_ok, cs_in, cT_ps, cT_ok, u_ps, u_ok,
         co_out) = (sem(n) for n in names)
        dve3, act3 = sem("dve3"), sem("act3")
        sq_ok, ss_ps, sd2_ok, ya_ok = sem("sq_ok"), sem("ss_ps"), sem("sd2_ok"), sem("ya_ok")
        sq = tile("sq", [P, 2, PIECE])
        sd = tile("sd", [P, 2, PIECE])
        state_in = a["state_hgrn"].rearrange("l b h d v -> d (l b) h v")
        state_out = o["hgrn_sample"].rearrange("l b h d v -> d (l b) h v")
        in_s, out_s = (in0, in1), (out0, out1)
        norm_items = [(h, n) for h in range(H) for n in range(PIECES)]
        with nc.Block() as block:
            @block.sync
            def _(sp):
                sp.dma_start(cst[:], a["state_conv"].rearrange("l b j w -> (l b j) w")).then_inc(cs_in, 16)
                sp.dma_start(o["conv_sample"][:, :, 0, :], a["state_conv"][:, :, 1, :]).then_inc(co_out, 16)

                def store(b):
                    sp.dma_start(state_out[:, b], snew[:, b % 2, :].rearrange("p (h v) -> p h v", h=H)).then_inc(
                        out_s[b % 2], 16)

                def next_weights(t):
                    sp.wait_ge(gate_ps, (t - 1) * PIECES)
                    load_gate(sp, t, t % 2)

                for b in range(NS):
                    if b >= 2:
                        sp.wait_ge(new_ok, b - 1)
                    sp.dma_start(sin[:, b % 2, :].rearrange("p (h v) -> p h v", h=H),
                                 state_in[:, b]).then_inc(in_s[b % 2], 16)
                    if b >= 2:
                        store(b - 2)
                    if b % PIECES == 1 and b > 1:
                        next_weights(GROUPS + 1 + b // PIECES)
                for b in range(NS - 2, NS):
                    sp.wait_ge(new_ok, b + 1)
                    store(b)
                for t in range(GROUPS + 2 + NS // PIECES, 2 * GROUPS):
                    next_weights(t)
                sp.wait_ge(u_ok, 1)
                sp.dma_start(o["conv_prompt"].rearrange("l b j w -> (l b j) w"), cso[0:2, :]).then_inc(co_out, 16)
                sp.dma_start(o["conv_sample"][0, :, 1, :], cso[2:, :]).then_inc(co_out, 16)
                sp.wait_ge(co_out, 48)
                for b in range(2):
                    sp.wait_ge(out_s[b], 16 * NS // 2)

            @block.gpsimd
            def _(pool):
                pool.memset(sel[:], 0.0).then_inc(sel0, 1)
                pool.wait_ge(sel0, 1)
                pool.affine_select(out=sel[:], in_=sel[:], compare_op=ALU.not_equal, fill=1.0, base=0,
                                   pattern=[[-1, NS], [0, P]], channel_multiplier=1).then_inc(sel_ok, 1)
                with pool.Fori(GROUPS, 2 * GROUPS) as t:
                    store_gate(pool, t)

            @block.tensor
            def _(pe):
                pe.wait_ge(sel_ok, 1)

                def value_rows(b):
                    if b >= 2:
                        pe.wait_ge(new_ok, b - 1)
                    pe.matmul(banks[b % 2][:], sel[:, b, :], vv[0:NS, TILES - 1, :], start=True,
                              stop=True).then_inc(vb_ps, 1)

                gate = iter([(t, n) for t in range(GROUPS, 2 * GROUPS) for n in range(PIECES)])

                def next_gate():
                    t, n = next(gate)
                    gate_product(pe, t, t % 2, n)

                value_rows(0)
                pe.wait_ge(cs_in, 16)
                for c in range(CH):
                    last = pe.transpose(banks[3][:, c * 2 * NS:(c + 1) * 2 * NS], cst[:, c * P:(c + 1) * P],
                                        ident[0:2 * NS, 0:2 * NS])
                last.then_inc(cT_ps, 1)
                for c in range(CH):
                    last = pe.transpose(banks[4][0:NS + 2, c * P:(c + 1) * P], cvT[:, c, T - 2:TT], ident[:])
                last.then_inc(u_ps, 1)
                for b in range(NS):
                    if b + 1 < NS:
                        value_rows(b + 1)
                    next_gate()
                    pe.wait_ge(new_ok, b + 1)
                    for h in range(H):
                        last = pe.matmul(banks[2][:, h * NS + b:h * NS + b + 1], snew[:, b % 2, h * HK:(h + 1) * HK],
                                         qT[:, h, T + b:T + b + 1], start=True, stop=True)
                    last.then_inc(os_ps, 1)
                for _ in range(GROUPS * PIECES - NS - len(norm_items)):
                    next_gate()
                for r, (h, n) in enumerate(norm_items):
                    next_gate()
                    pe.wait_ge(sq_ok, r + 1)
                    if r >= 2:
                        pe.wait_ge(sd2_ok, r - 1)
                    pe.matmul(banks[5 + r % 2][:, 0:PIECE], onesm[:], sq[:, r % 2, :], start=True, stop=True).then_inc(ss_ps, 1)

            @block.scalar
            def _(act):
                act.wait_ge(cT_ps, 1)
                act.activation(cstT[:].rearrange("p c n -> p (c n)"), banks[3][:, 0:CH * 2 * NS], ACT.Copy).then_inc(cT_ok, 1)
                act.wait_ge(u_ps, 1)
                act.activation(cso[:], banks[4][0:NS + 2, :], ACT.Copy).then_inc(u_ok, 1)
                gate = iter([(t, n) for t in range(GROUPS, 2 * GROUPS) for n in range(PIECES)])
                for _ in range(NS):
                    take_gate(act, *next(gate))
                act.wait_ge(os_ps, NS)
                act.activation(qT[:, :, T:], banks[2][:, 0:H * NS].rearrange("p (h b) -> p h b", h=H), ACT.Copy).then_inc(os_ok, 1)
                act.wait_ge(os_ok, 1)
                for _ in range(GROUPS * PIECES - NS - len(norm_items)):
                    take_gate(act, *next(gate))
                for r, (h, n) in enumerate(norm_items):
                    at = slice(n * PIECE, (n + 1) * PIECE)
                    if r >= 2:
                        act.wait_ge(ss_ps, r - 1)
                    act.activation(sq[:, r % 2, :], qT[:, h, at], ACT.Square).then_inc(sq_ok, 1)
                    take_gate(act, *next(gate))
                    act.wait_ge(ss_ps, r + 1)
                    if r >= 2:
                        act.wait_ge(ya_ok, r - 1)
                    act.activation(sd[:, r % 2, :], banks[5 + r % 2][:, 0:PIECE], ACT.Sqrt, scale=1.0 / HK,
                                   bias=eps[:, 0:1]).then_inc(sd2_ok, 1)

            @block.vector
            def _(dve):
                s = Steps(dve, dve3)
                s.link(dve.tensor_scalar(ks[:], fT[:, :, T:], -1.0, 1.0, ALU.mult, ALU.add))
                for b in range(NS):
                    dve.wait_ge(in_s[b % 2], 16 * (b // 2 + 1))
                    if b >= 2:
                        dve.wait_ge(out_s[b % 2], 16 * (b // 2))
                        dve.wait_ge(os_ps, b - 1)
                    dve.wait_ge(vb_ps, b + 1)

                    def h3b(x):
                        return x.rearrange("p (h v) -> p h v", h=H)

                    s.run(dve.tensor_tensor(h3b(snew[:, b % 2]), h3b(sin[:, b % 2]),
                                            fT[:, :, T + b:T + b + 1].to_broadcast([P, H, HK]), ALU.mult))
                    s.run(dve.tensor_tensor(h3b(stmp[:]), h3b(banks[b % 2][:]),
                                            ks[:, :, b:b + 1].to_broadcast([P, H, HK]), ALU.mult))
                    s.settle()
                    dve.tensor_tensor(snew[:, b % 2], snew[:, b % 2], stmp[:], ALU.add).then_inc(new_ok, 1)
                    dve.wait_ge(new_ok, b + 1)
                dve.wait_ge(cT_ok, 1)
                for c in range(CH):
                    w0, w1, w2 = (par[:, O_CW + j * CH + c:O_CW + j * CH + c + 1] for j in range(3))
                    bias = par[:, O_CB + c:O_CB + c + 1]
                    u = cvT[:, c, :]
                    s.link(dve.tensor_scalar(conv[:], u[:, 0:T], w2, bias, ALU.mult, ALU.add))
                    s.link(dve.scalar_tensor_tensor(out=conv[:, 1:], in0=u[:, 0:T - 1], scalar=w1, in1=conv[:, 1:],
                                                    op0=ALU.mult, op1=ALU.add))
                    s.link(dve.scalar_tensor_tensor(out=conv[:, 2:], in0=u[:, 0:T - 2], scalar=w0, in1=conv[:, 2:],
                                                    op0=ALU.mult, op1=ALU.add))
                    s.run(dve.tensor_tensor(bT[:, c, 0:T], bT[:, c, 0:T], conv[:], ALU.mult))
                    old = cstT[:, c, :].rearrange("p (b j) -> p b j", j=2)
                    s.link(dve.tensor_scalar(stmp[:, 0:NS], u[:, T:], w2, bias, ALU.mult, ALU.add))
                    s.link(dve.scalar_tensor_tensor(out=stmp[:, 0:NS], in0=old[:, :, 1], scalar=w1, in1=stmp[:, 0:NS],
                                                    op0=ALU.mult, op1=ALU.add))
                    s.link(dve.scalar_tensor_tensor(out=stmp[:, 0:NS], in0=old[:, :, 0], scalar=w0, in1=stmp[:, 0:NS],
                                                    op0=ALU.mult, op1=ALU.add))
                    s.link(dve.tensor_tensor(bT[:, c, T:], bT[:, c, T:], stmp[:, 0:NS], ALU.mult))
                for r, (h, n) in enumerate(norm_items):
                    at = slice(n * PIECE, (n + 1) * PIECE)
                    dve.wait_ge(sd2_ok, r + 1)
                    s.link(dve.reciprocal(sd[:, r % 2, :], sd[:, r % 2, :]))
                    s.link(dve.scalar_tensor_tensor(out=sd[:, r % 2, :], in0=sd[:, r % 2, :],
                                                    scalar=par[:, O_HG + h:O_HG + h + 1], in1=gT[:, h, at],
                                                    op0=ALU.mult, op1=ALU.mult))
                    dve.tensor_tensor(qT[:, h, at], qT[:, h, at], sd[:, r % 2, :], ALU.mult).then_inc(ya_ok, 1)


def merge(nc, a, sb, sem, banks, gates_d, yaT, ybT, mT):
    with ExitStack() as ctx:
        wo = [sb(f"wo{j}", [P, 2, CH, P], ctx=ctx) for j in range(2)]
        gate = [sb(f"gate{j}", [P, 2, TT], ctx=ctx) for j in range(2)]
        part = sb("part", [P, 2, 2, PIECE], ctx=ctx)
        w_ok = [sem("mg_w0"), sem("mg_w1")]
        outs_ps, gates_ok, free, part_ok = (sem(n) for n in ("mg_op", "mg_go", "mg_free", "mg_part"))
        out_w = [a[n].rearrange("l (k p) n -> p (l k) n", p=P) for n in ("w_out_hgrn", "w_out_conv")]
        with nc.Block() as block:
            @block.sync
            def _(sp):
                def load(t, j):
                    for x in range(2):
                        sp.dma_start(wo[j][:, x], out_w[x][:, :, bass.ds(t * P, P)]).then_inc(w_ok[j], 16)
                        sp.dma_start(gate[j][:, x, :], gates_d[bass.ds(t + x * KD, 1)].rearrange(
                            "a p t -> p (a t)")).then_inc(w_ok[j], 16)

                for j in range(2):
                    load(j, j)
                with sp.Fori(1, KD // 2) as i:
                    for j in range(2):
                        sp.wait_ge(free, (2 * i - 1 + j) * PIECES + 3)
                        load(2 * i + j, j)

            @block.tensor
            def _(pe):
                with pe.Fori(0, KD // 2) as i:
                    for r in range(2 * PIECES):
                        j, n = divmod(r, PIECES)
                        toks = slice(n * PIECE, (n + 1) * PIECE)
                        if n == 0:
                            pe.wait_ge(w_ok[j], 64 * i + 64)
                        pe.wait_ge(free, i * (2 * PIECES) + r + 1)
                        for x, y in enumerate((yaT, ybT)):
                            for k in range(CH):
                                last = pe.matmul(banks[2 * (r % 3) + x][:, 0:PIECE], wo[j][:, x, k, :], y[:, k, toks],
                                                 start=(k == 0), stop=(k == CH - 1))
                        last.then_inc(outs_ps, 1)

            @block.scalar
            def _(act):
                with act.Fori(0, KD // 2) as i:
                    for j in range(2):
                        act.wait_ge(w_ok[j], 64 * i + 64)
                        act.activation(gate[j][:], gate[j][:], ACT.Sigmoid).then_inc(gates_ok, 1)

            @block.vector
            def _(dve):
                dve.sem_inc(free, 3)
                with dve.Fori(0, KD // 2) as i:
                    for r in range(2 * PIECES):
                        j, n = divmod(r, PIECES)
                        toks = slice(n * PIECE, (n + 1) * PIECE)
                        done = i * (2 * PIECES) + r
                        if n == 0:
                            dve.wait_ge(gates_ok, 2 * i + j + 1)
                        dve.wait_ge(outs_ps, done + 1)
                        for x in range(2):
                            dve.tensor_tensor(part[:, r % 2, x, :], banks[2 * (r % 3) + x][:, 0:PIECE],
                                              gate[j][:, x, toks], ALU.mult).then_inc(part_ok, 1)
                        dve.wait_ge(part_ok, 2 * done + 2)
                        dve.tensor_tensor(mT[:, bass.ds(2 * i + j, 1), toks].rearrange("p a n -> p (a n)"),
                                          part[:, r % 2, 0, :], part[:, r % 2, 1, :], ALU.add).then_inc(free, 1)


def output_and_norm(nc, a, sb, sem, banks, ident, eps, mod_d, x2_d, xe_d, x_rows, mT, h2T):
    with ExitStack() as ctx:
        def tile(name, shape, dt=F32):
            return sb(name, shape, dt, ctx)

        wo = tile("wo", [P, KD, D])
        cond = tile("cond", [P, 3, D])
        cond_s = tile("cond_s", [NS, 3, D])
        gff = tile("gff", [P, D])
        xt = tile("xt", [P, 2, D])
        x2 = tile("x2", [P, 2, D])
        h2 = tile("h2", [P, 2, D])
        sqj = tile("sqj", [P, D])
        st = tile("st", [P, 4])
        names = "w4 c4 x4 mm4 x2ok sq4 r4 h4 st4 tp4 ev4 a4".split()
        wo_in, cond_in, _, mm, x2_ok, sq_ok, sd_ok, h2_ok, _, tp, ev, a_ok = (sem("s4" + n) for n in names)
        x_in = [sem("s4x0"), sem("s4x1")]
        stored = [sem("s4o0"), sem("s4o1")]
        dve4 = sem("dve4")
        with nc.Block() as block:
            @block.sync
            def _(sp):
                sp.dma_start(wo[:], a["w_o"].rearrange("l (k p) n -> p (l k) n", p=P)).then_inc(wo_in, 16)
                for j, m in enumerate((2, 4, 3)):
                    sp.dma_start(cond[:, j, :], mod_d[NS:NS + 1, m * D:(m + 1) * D].to_broadcast([P, D])).then_inc(cond_in, 16)
                    sp.dma_start(cond_s[:, j, :], mod_d[0:NS, m * D:(m + 1) * D]).then_inc(cond_in, 16)
                sp.dma_start(gff[:], a["norm_ffn_g"].to_broadcast([P, D])).then_inc(cond_in, 16)
                for t in range(TILES):
                    r = rows_of(t)
                    sp.wait_ge(x2_ok, t + 1)
                    sp.dma_start(x2_d[t * P:t * P + r, :], x2[0:r, t % 2, :]).then_inc(stored[t % 2], 16)
                    sp.wait_ge(h2_ok, t + 1)
                    sp.dma_start(xe_d[ROW0 + t * P:ROW0 + t * P + r, 0:D], h2[0:r, t % 2, :]).then_inc(stored[t % 2], 16)
                for b in range(2):
                    sp.wait_ge(stored[b], 32 * ((TILES + 1 - b) // 2))

            @block.gpsimd
            def _(pool):
                for t in range(TILES):
                    if t >= 2:
                        pool.wait_ge(x2_ok, t - 1)
                    pool.dma_start(xt[0:rows_of(t), t % 2, :], x_rows(t)).then_inc(x_in[t % 2], 16)

            @block.tensor
            def _(pe):
                pe.wait_ge(wo_in, 16)

                def product(t):
                    if t >= 2:
                        pe.wait_ge(x2_ok, t - 1)
                    r = rows_of(t)
                    for half in range(2):
                        for k in range(KD):
                            last = pe.matmul(banks[2 * (t % 2) + half][0:r, :], mT[:, k, t * P:t * P + r],
                                             wo[:, k, half * 512:(half + 1) * 512], start=(k == 0), stop=(k == KD - 1))
                    last.then_inc(mm, 1)

                def turn(t):
                    r = rows_of(t)
                    pe.wait_ge(h2_ok, t + 1)
                    if t >= 2:
                        pe.wait_ge(ev, 2 * t - 2)
                    for k in range(KD):
                        last = pe.transpose(banks[4 + 2 * (t % 2) + k // 4][:, (k % 4) * P:(k % 4) * P + r],
                                            h2[0:r, t % 2, k * P:(k + 1) * P], ident[0:r, 0:r])
                    last.then_inc(tp, 1)

                product(0)
                for t in range(TILES):
                    if t + 1 < TILES:
                        product(t + 1)
                    turn(t)

            @block.scalar
            def _(act):
                def square(t):
                    r = rows_of(t)
                    act.wait_ge(x2_ok, t + 1)
                    if t:
                        act.wait_ge(h2_ok, t)
                    act.activation(sqj[0:r, :], x2[0:r, t % 2, :], ACT.Square, accum_out=st[0:r, 0:1]).then_inc(sq_ok, 1)
                    act.wait_ge(sq_ok, t + 1)
                    act.activation(st[0:r, 1:2], st[0:r, 0:1], ACT.Sqrt, scale=1.0 / D, bias=eps[0:r, 0:1]).then_inc(sd_ok, 1)

                def take(t):
                    r = rows_of(t)
                    act.wait_ge(tp, t + 1)
                    for half in range(2):
                        act.activation(h2T[:, 4 * half:4 * half + 4, t * P:t * P + r],
                                       banks[4 + 2 * (t % 2) + half][:].rearrange("p (k n) -> p k n", n=P)[:, :, 0:r],
                                       ACT.Copy).then_inc(ev, 1)

                for t in range(TILES):
                    square(t)
                    take(t)

            @block.vector
            def _(dve):
                s = Steps(dve, dve4)
                dve.wait_ge(cond_in, 16 * 7)
                s.run(dve.scalar_tensor_tensor(out=cond[:, 1, :], in0=cond[:, 1, :], scalar=1.0, in1=gff[:], op0=ALU.add, op1=ALU.mult))
                s.run(dve.scalar_tensor_tensor(out=cond_s[:, 1, :], in0=cond_s[:, 1, :], scalar=1.0, in1=gff[0:NS, :], op0=ALU.add, op1=ALU.mult))
                s.settle()
                for t in range(TILES):
                    r = rows_of(t)
                    c = (cond if t < TILES - 1 else cond_s)[0:r]
                    dve.wait_ge(mm, t + 1)
                    dve.wait_ge(x_in[t % 2], 16 * (t // 2 + 1))
                    if t >= 2:
                        dve.wait_ge(stored[t % 2], 32 * (t // 2))
                    for half in range(2):
                        at = slice(512 * half, 512 * half + 512)
                        s.run(dve.tensor_tensor(x2[0:r, t % 2, at], banks[2 * (t % 2) + half][0:r, :], c[:, 0, at], ALU.mult))
                    s.settle()
                    dve.tensor_tensor(x2[0:r, t % 2, :], x2[0:r, t % 2, :], xt[0:r, t % 2, :], ALU.add).then_inc(x2_ok, 1)
                    dve.wait_ge(sd_ok, t + 1)
                    s.link(dve.reciprocal(st[0:r, 2:3], st[0:r, 1:2]))
                    if t >= 2:
                        dve.wait_ge(tp, t - 1)
                    s.link(dve.scalar_tensor_tensor(out=h2[0:r, t % 2, :], in0=x2[0:r, t % 2, :], scalar=st[0:r, 2:3],
                                                    in1=c[:, 1, :], op0=ALU.mult, op1=ALU.mult))
                    dve.tensor_tensor(h2[0:r, t % 2, :], h2[0:r, t % 2, :], c[:, 2, :], ALU.add).then_inc(h2_ok, 1)


def routing(nc, a, sb, sem, banks, hT, xe_d, acc_d, posm, table, total, tok, idle, iota, wexp, slot_in):
    with ExitStack() as ctx:
        def tile(name, shape, dt=F32):
            return sb(name, shape, dt, ctx)

        wr = tile("wr", [P, KD, E])
        wsh = tile("wsh", [P, KD, 2 * FF])
        wsd = tile("wsd", [P, FF // P, D])
        sg = tile("sgs", [P, 2, PIECE])
        hs = tile("hs", [P, FF // P, TT])
        ysh = tile("ysh", [P, 2, D])
        zero = tile("zero", [P, XW // 2])
        rb = tile("rb", [P, E])
        sc = tile("sc", [P, TILES, E])
        sel = tile("selr", [P, TILES, E])
        top8 = tile("top8", [P, TILES * EG, 8])
        gs = tile("gs", [P, TILES, EG])
        gt = tile("gt", [P, TILES, EG, EG])
        eq = tile("eq", [P, TILES, EG, EG])
        lower = tile("lower", [P, EG, EG])
        gok = tile("gok", [P, TILES, EG])
        pen = tile("pen", [P, TILES, EG])
        mask = tile("mask", [P, TILES, E])
        maskb = tile("maskb", [P, TILES, E], BF16)
        wsum = tile("wsum", [P, TILES])
        wts = eq[:].rearrange("p t a b -> p t (a b)")
        base = gt[:].rearrange("p t a b -> p t (a b)")
        tri = tile("tri", [P, P], BF16)
        trii = tile("trii", [P, P], BF16)
        onesb = tile("onesb", [P, P], BF16)
        thr = tile("thr", [P, 8])
        thj = tile("thj", [E, 8])
        nb = tile("nb", [E, 4])
        nbb = tile("nbb", [E, 2], BF16)
        past = tile("past", [E, ITEMS + AHEAD], BF16)
        tf = tile("tf", [1, 2, ITEMS + AHEAD])
        names = ("w_in b_in lg sc mk pf tot cnt nb incl past tab wt const z "
                 "gps gok ups hok dps yok").split()
        (w_ok, rb_ok, lg_ps, sc_ok, mk_ok, pf_ps, _, cnt_ps, nb_ok, incl_ps, past_ok, tab_ps, wt_ok, const_ok, z_ok,
         g_ps, g_ok, u_ps, h_ok, d_ps, y_ok) = (sem("s5" + n) for n in names)
        dve5, pool5 = sem("dve5"), sem("pool5")
        stored = [sem("s5y0"), sem("s5y1"), sem("s5w")]
        sh_in = sem("s5sh")
        pieces = [(f, n) for f in range(FF // P) for n in range(PIECES)]
        FULL = TILES - 1
        with nc.Block() as block:
            @block.sync
            def _(sp):
                sp.dma_start(wr[:], a["w_router"].rearrange("l (k p) n -> p (l k) n", p=P)).then_inc(w_ok, 16)
                sp.dma_start(rb[:], a["router_bias"].to_broadcast([P, E])).then_inc(rb_ok, 16)
                sp.dma_start(wsh[:, :, 0:FF], a["w_sh_gate"].rearrange("l (k p) n -> p (l k) n", p=P)).then_inc(sh_in, 16)
                sp.dma_start(wsh[:, :, FF:], a["w_sh_up"].rearrange("l (k p) n -> p (l k) n", p=P)).then_inc(sh_in, 16)
                sp.dma_start(wsd[:], a["w_sh_down"].rearrange("l (k p) n -> p (l k) n", p=P)).then_inc(sh_in, 16)
                for e in range(2):
                    load_expert(sp, a, wexp, e, e, slot_in[e])
                sp.wait_ge(z_ok, 1)
                for c in range(2):
                    sp.dma_start(xe_d[0:ROW0, c * (XW // 2):(c + 1) * (XW // 2)], zero[0:ROW0, :]).then_inc(stored[2], 16)
                    sp.dma_start(acc_d[0:ROW0, c * (D // 2):(c + 1) * (D // 2)], zero[0:ROW0, 0:D // 2]).then_inc(stored[2], 16)
                    sp.dma_start(xe_d[ROW0 + TT:, c * (XW // 2):(c + 1) * (XW // 2)], zero[:]).then_inc(stored[2], 16)
                sp.wait_ge(wt_ok, 1)
                for t in range(TILES):
                    r = rows_of(t)
                    sp.dma_start(xe_d[ROW0 + t * P:ROW0 + t * P + r, D:], wts[0:r, t, :]).then_inc(stored[2], 16)
                for t in range(TILES):
                    r = rows_of(t)
                    sp.wait_ge(y_ok, 2 * t + 2)
                    sp.dma_start(acc_d[ROW0 + t * P:ROW0 + t * P + r, :], ysh[0:r, t % 2, :]).then_inc(stored[t % 2], 16)
                sp.wait_ge(stored[2], 16 * (TILES + 6))
                for b in range(2):
                    sp.wait_ge(stored[b], 16 * ((TILES + 1 - b) // 2))

            @block.gpsimd
            def _(pool):
                pool.memset(zero[:], 0.0).then_inc(z_ok, 1)
                pool.memset(tri[:], 1.0).then_inc(pool5, 1)
                pool.memset(trii[:], 1.0).then_inc(pool5, 1)
                pool.memset(lower[:], 1.0).then_inc(pool5, 1)
                pool.memset(onesb[:], 1.0).then_inc(const_ok, 1)
                pool.memset(posm[:], -1.0).then_inc(const_ok, 1)
                pool.memset(mask[:, FULL, :], 0.0).then_inc(const_ok, 1)
                pool.memset(sc[:, FULL, :], 0.0).then_inc(const_ok, 1)
                pool.iota(iota[:], [[1, TILES * P]], base=0, channel_multiplier=0,
                          allow_small_or_imprecise_dtypes=True).then_inc(const_ok, 1)
                pool.iota(idle[:], [[0, 1]], base=ROW0 + TT, channel_multiplier=1,
                          allow_small_or_imprecise_dtypes=True).then_inc(const_ok, 1)
                pool.iota(tok[:, :, 0:1], [[0, TILES], [0, 1]], base=ROW0, channel_multiplier=1,
                          allow_small_or_imprecise_dtypes=True).then_inc(const_ok, 1)
                pool.iota(tok[:, :, 1:2], [[P, TILES], [0, 1]], base=0, channel_multiplier=0,
                          allow_small_or_imprecise_dtypes=True).then_inc(const_ok, 1)
                pool.iota(thr[:], [[P, 8]], base=P, channel_multiplier=0,
                          allow_small_or_imprecise_dtypes=True).then_inc(const_ok, 1)
                pool.wait_ge(pool5, 3)
                pool.affine_select(out=tri[:], in_=tri[:], compare_op=ALU.is_gt, fill=0.0, base=0,
                                   pattern=[[1, P]], channel_multiplier=-1).then_inc(const_ok, 1)
                pool.affine_select(out=trii[:], in_=trii[:], compare_op=ALU.is_ge, fill=0.0, base=0,
                                   pattern=[[1, P]], channel_multiplier=-1).then_inc(const_ok, 1)
                pool.affine_select(out=lower[:], in_=lower[:], compare_op=ALU.is_gt, fill=0.0, base=0,
                                   pattern=[[1, EG], [-1, EG]], channel_multiplier=0).then_inc(const_ok, 1)
                for r, (f, n) in enumerate(pieces):
                    pool.wait_ge(g_ok, 2 * r + 2)
                    at = hs[:, f, n * PIECE:(n + 1) * PIECE]
                    pool.tensor_tensor(at, at, sg[:, r % 2, :], ALU.mult).then_inc(h_ok, 1)

            CONST = 12

            @block.tensor
            def _(pe):
                pe.wait_ge(w_ok, 16)
                for t in range(TILES):
                    r = rows_of(t)
                    bank, at = (0, t * E) if t < 5 else (1, (t - 5) * E)
                    for k in range(KD):
                        last = pe.matmul(banks[bank][0:r, at:at + E], hT[:, k, t * P:t * P + r], wr[:, k, :],
                                         start=(k == 0), stop=(k == KD - 1))
                last.then_inc(lg_ps, 1)
                pe.wait_ge(sh_in, 48)
                for r, (f, n) in enumerate(pieces):
                    toks = slice(n * PIECE, (n + 1) * PIECE)
                    if r >= 1:
                        pe.wait_ge(g_ok, 2 * r)
                    for half in range(2):
                        for k in range(KD):
                            last = pe.matmul(banks[2 + half][:, 0:PIECE], wsh[:, k, half * FF + f * P:half * FF + (f + 1) * P],
                                             hT[:, k, toks], start=(k == 0), stop=(k == KD - 1))
                    last.then_inc(g_ps, 1)
                pe.wait_ge(const_ok, CONST)
                pe.wait_ge(mk_ok, 1)
                pe.matmul(banks[0][:], tri[:], maskb[:, 0:FULL, :].rearrange("p t e -> p (t e)"), start=True, stop=True)
                pe.matmul(banks[4][0:NS, 0:E], tri[0:NS, 0:NS], maskb[0:NS, FULL, :], start=True, stop=True)
                pe.matmul(banks[1][:], onesb[:], maskb[:, 0:FULL, :].rearrange("p t e -> p (t e)"), start=True,
                          stop=True).then_inc(pf_ps, 1)
                for t in range(TILES):
                    last = pe.matmul(banks[5][0:E, 0:1], maskb[:, t, :], onesb[:, 0:1], start=(t == 0), stop=(t == TILES - 1))
                last.then_inc(cnt_ps, 1)
                pe.wait_ge(nb_ok, 1)
                pe.matmul(banks[6][0:E, 0:1], trii[0:E, 0:E], nbb[:, 0:1], start=True, stop=True).then_inc(incl_ps, 1)
                pe.wait_ge(past_ok, 1)
                n = ITEMS + AHEAD
                pe.matmul(banks[7][0:1, 0:n], onesb[0:E, 0:1], past[:], start=True, stop=True)
                pe.matmul(banks[7][0:1, 256:256 + n], nbb[:, 0:1], past[:], start=True, stop=True)
                pe.matmul(banks[7][0:1, 500:501], nbb[:, 0:1], onesb[0:E, 0:1], start=True, stop=True).then_inc(tab_ps, 1)
                pe.wait_ge(h_ok, len(pieces))
                for t in range(TILES):
                    r = rows_of(t)
                    for half in range(2):
                        if t >= 1:
                            pe.wait_ge(y_ok, 2 * t - 1 + half)
                        for f in range(FF // P):
                            last = pe.matmul(banks[2 + half][0:r, :], hs[:, f, t * P:t * P + r],
                                             wsd[:, f, half * 512:(half + 1) * 512], start=(f == 0), stop=(f == FF // P - 1))
                        last.then_inc(d_ps, 1)

            @block.scalar
            def _(act):
                act.wait_ge(const_ok, CONST)
                act.wait_ge(lg_ps, 1)
                act.activation(sc[:, 0:5, :].rearrange("p t e -> p (t e)"), banks[0][:, 0:5 * E], ACT.Sigmoid).then_inc(sc_ok, 1)
                act.activation(sc[:, 5:FULL, :].rearrange("p t e -> p (t e)"), banks[1][:, 0:3 * E], ACT.Sigmoid).then_inc(sc_ok, 1)
                act.activation(sc[0:NS, FULL, :], banks[1][0:NS, 3 * E:4 * E], ACT.Sigmoid).then_inc(sc_ok, 1)
                for r, (f, n) in enumerate(pieces):
                    act.wait_ge(g_ps, r + 1)
                    if r >= 2:
                        act.wait_ge(h_ok, r - 1)
                    act.activation(sg[:, r % 2, :], banks[2][:, 0:PIECE], ACT.Silu).then_inc(g_ok, 1)
                    act.activation(hs[:, f, n * PIECE:(n + 1) * PIECE], banks[3][:, 0:PIECE], ACT.Copy).then_inc(g_ok, 1)
                for t in range(TILES):
                    r = rows_of(t)
                    if t >= 2:
                        act.wait_ge(stored[t % 2], 16 * (t // 2))
                    for half in range(2):
                        act.wait_ge(d_ps, 2 * t + half + 1)
                        act.activation(ysh[0:r, t % 2, half * 512:(half + 1) * 512], banks[2 + half][0:r, :],
                                       ACT.Copy).then_inc(y_ok, 1)

            @block.vector
            def _(dve):
                s = Steps(dve, dve5)
                dve.wait_ge(rb_ok, 16)
                dve.wait_ge(sc_ok, 3)
                dve.wait_ge(const_ok, CONST)
                s.link(dve.tensor_tensor(sel[:], sc[:], rb[:].unsqueeze(1).to_broadcast([P, TILES, E]), ALU.add))
                for t in range(TILES):
                    for g in range(EG):
                        s.run(dve.max(top8[:, t * EG + g, :], sel[:, t, g * EG:(g + 1) * EG]))
                s.settle()
                s.link(dve.tensor_tensor(gs[:].rearrange("p t g -> p (t g)"), top8[:, :, 0], top8[:, :, 1], ALU.add))
                this = gs[:].unsqueeze(3).to_broadcast([P, TILES, EG, EG])
                other = gs[:].unsqueeze(2).to_broadcast([P, TILES, EG, EG])
                s.run(dve.tensor_tensor(gt[:], other, this, ALU.is_gt))
                s.link(dve.tensor_tensor(eq[:], other, this, ALU.is_equal))
                s.link(dve.tensor_tensor(eq[:], eq[:], lower[:].unsqueeze(1).to_broadcast([P, TILES, EG, EG]), ALU.mult))
                s.link(dve.tensor_tensor(gt[:], gt[:], eq[:], ALU.add))
                s.link(dve.tensor_reduce(pen[:], gt[:], AX.X, ALU.add))
                s.link(dve.tensor_scalar(gok[:], pen[:], float(TOPG), None, ALU.is_lt))
                s.link(dve.tensor_scalar(pen[:], gok[:], -NEG, NEG, ALU.mult, ALU.add))
                sel4 = sel[:].rearrange("p t (g e) -> p t g e", e=EG)
                s.link(dve.tensor_tensor(sel4, sel4, gok[:].unsqueeze(3).to_broadcast([P, TILES, EG, EG]), ALU.mult))
                s.link(dve.tensor_tensor(sel4, sel4, pen[:].unsqueeze(3).to_broadcast([P, TILES, EG, EG]), ALU.add))
                for t in range(TILES):
                    s.run(dve.max(top8[:, t, :], sel[:, t, :]))
                s.settle()
                for t in range(TILES):
                    s.run(dve.match_replace(wts[:, t, :], top8[:, t, :], sel[:, t, :], 2 * NEG))
                s.settle()
                s.run(dve.tensor_scalar(mask[:, 0:FULL, :], wts[:, 0:FULL, :], 1.5 * NEG, None, ALU.is_lt))
                s.link(dve.tensor_scalar(mask[0:NS, FULL, :], wts[0:NS, FULL, :], 1.5 * NEG, None, ALU.is_lt))
                dve.tensor_copy(maskb[:], mask[:]).then_inc(mk_ok, 1)
                s.link(dve.tensor_tensor(wts, sc[:], mask[:], ALU.mult))
                s.run(dve.tensor_reduce(wsum[:, 0:FULL], wts[:, 0:FULL, :], AX.X, ALU.add))
                s.link(dve.tensor_reduce(wsum[0:NS, FULL:], wts[0:NS, FULL:, :], AX.X, ALU.add))
                s.run(dve.reciprocal(wsum[:, 0:FULL], wsum[:, 0:FULL]))
                s.link(dve.reciprocal(wsum[0:NS, FULL:], wsum[0:NS, FULL:]))
                s.run(dve.tensor_scalar(wsum[:, 0:FULL], wsum[:, 0:FULL], SCALE, None, ALU.mult))
                s.link(dve.tensor_scalar(wsum[0:NS, FULL:], wsum[0:NS, FULL:], SCALE, None, ALU.mult))
                s.run(dve.tensor_tensor(wts[:, 0:FULL, :], wts[:, 0:FULL, :],
                                        wsum[:, 0:FULL].unsqueeze(2).to_broadcast([P, FULL, E]), ALU.mult))
                s.link(dve.tensor_scalar(wts[0:NS, FULL, :], wts[0:NS, FULL, :], wsum[0:NS, FULL:], None, ALU.mult))
                dve.sem_inc(wt_ok, 1)
                s.run(dve.memset(base[:, 0, :], 0.0))
                dve.wait_ge(pf_ps, 1)
                for t in range(1, TILES):
                    s.settle()
                    s.run(dve.tensor_tensor(base[:, t, :], base[:, t - 1, :], banks[1][:, (t - 1) * E:t * E], ALU.add))
                s.settle()
                s.run(dve.tensor_tensor(base[:, 0:FULL, :], base[:, 0:FULL, :],
                                        banks[0][:].rearrange("p (t e) -> p t e", e=E), ALU.add))
                s.link(dve.tensor_tensor(base[0:NS, FULL, :], base[0:NS, FULL, :], banks[4][0:NS, 0:E], ALU.add))
                s.run(dve.scalar_tensor_tensor(out=base[:, 0:FULL, :], in0=base[:, 0:FULL, :], scalar=1.0,
                                               in1=mask[:, 0:FULL, :], op0=ALU.add, op1=ALU.mult))
                s.link(dve.scalar_tensor_tensor(out=base[0:NS, FULL, :], in0=base[0:NS, FULL, :], scalar=1.0,
                                                in1=mask[0:NS, FULL, :], op0=ALU.add, op1=ALU.mult))
                s.run(dve.tensor_scalar(posm[:, 0:E, 0:FULL], base[:, 0:FULL, :].rearrange("p t e -> p e t"), -1.0, None, ALU.add))
                s.run(dve.tensor_scalar(posm[0:NS, 0:E, FULL], base[0:NS, FULL, :], -1.0, None, ALU.add))
                dve.wait_ge(cnt_ps, 1)
                s.link(dve.tensor_copy(nb[:, 0:1], banks[5][0:E, 0:1]))
                s.link(dve.tensor_scalar(thj[:], thr[0:E, :], nb[:, 0:1], None, ALU.is_lt))
                s.link(dve.tensor_reduce(nb[:, 1:2], thj[:], AX.X, ALU.add))
                dve.tensor_scalar(nbb[:, 0:1], nb[:, 1:2], 1.0, None, ALU.add).then_inc(nb_ok, 1)
                dve.wait_ge(incl_ps, 1)
                s.link(dve.tensor_copy(nb[:, 2:3], banks[6][0:E, 0:1]))
                dve.tensor_scalar(past[:], iota[0:E, 0:ITEMS + AHEAD], nb[:, 2:3], None, ALU.is_ge).then_inc(past_ok, 1)
                dve.wait_ge(tab_ps, 1)
                n = ITEMS + AHEAD
                s.run(dve.tensor_copy(table[:, :, 0], banks[7][0:1, 0:n]))
                s.run(dve.tensor_copy(total[:], banks[7][0:1, 500:501]))
                s.link(dve.tensor_tensor(tf[:, 0, :], iota[0:1, 0:n], banks[7][0:1, 256:256 + n], ALU.subtract))
                s.link(dve.tensor_scalar(tf[:, 1, :], tf[:, 0, :], float(TILES - 1), float(P), ALU.min, ALU.mult))
                s.link(dve.tensor_scalar(tf[:, 0, :], banks[7][0:1, 0:n], float(E), float(P), ALU.is_ge, ALU.mult))
                s.link(dve.tensor_tensor(tf[:, 1, :], tf[:, 1, :], tf[:, 0, :], ALU.max))
                s.link(dve.tensor_copy(table[:, :, 1], tf[:, 1, :]))


def load_expert(eng, a, wexp, e, slot, landed):
    def src(name):
        return a[name][0, bass.ds(e, 1)].rearrange("e (k p) n -> p (e k) n", p=P)

    eng.dma_start(wexp[:, slot, 0:KD, 0:FF], src("w_exp_gate")).then_inc(landed, 16)
    eng.dma_start(wexp[:, slot, 0:KD, FF:], src("w_exp_up")).then_inc(landed, 16)
    eng.dma_start(wexp[:, slot, KD:, :].rearrange("p (k h) n -> p k (h n)", h=2), src("w_exp_down")).then_inc(landed, 16)


def experts(nc, a, sb, sem, banks, ident, xe_d, acc_d, posm, table, total, tok, idle, iota, wexp, slot_in):
    with ExitStack() as ctx:
        def tile(name, shape, dt=F32):
            return sb(name, shape, dt, ctx)

        xg = tile("xg", [P, 2, XW + 1])
        xT = tile("xT", [P, 2, KD, P])
        oh = tile("oh", [P, 2, TILES, P], BF16)
        sg = tile("sg", [P, FF])
        hh = tile("hh", [P, FF])
        hT = tile("hTe", [P, FF // P, P])
        ob = tile("ob", [P, 2, D])
        wcol = tile("wcol", [P, 2])
        none = tile("none", [P, D // 2])
        ixf = tile("ixf", [P, 4])
        lists = tile("lists", [P, LISTS], U32)
        ix = [tile(f"ix{b}", [P, 1], U32) for b in range(2)]
        ixs = [tile(f"ixs{b}", [P, 1], U32) for b in range(2)]
        names = "oh ixp ls ix ixs tp xT wc gu sg h hp hT dn ob scat w ent pad fin".split()
        (oh_ok, ix_ps, list_ok, ix_ok, ixs_ok, x_tp, xT_ok, wc_ok, gu_ps, sg_ok, h_ok, h_tp, hT_ok, dn_ps, ob_ok, added,
         w_ok, entered, pad_ok, _) = (sem("s6" + n) for n in names)
        gat = [sem("s6g0"), sem("s6g1")]
        passed = sem("s6passed")
        dve6 = sem("dve6")

        def entry(eng, i, field, top):
            return eng.value_load(table[0:1, bass.ds(i, 1), field:field + 1].rearrange("a b c -> a (b c)"),
                                  min_val=0, max_val=top)

        def blocks(eng, body, enter=None, leave=None):
            with eng.Fori(0, ITEMS // SPAN) as span:
                with eng.If(entry(eng, span * SPAN, 0, E) < E):
                    with eng.Fori(0, SPAN // 2) as part:
                        it = span * (SPAN // 2) + part
                        if enter:
                            enter(it)
                        for b in range(2):
                            i = it * 2 + b
                            with eng.If(entry(eng, i, 0, E) < E):
                                body(i, b)
                            eng.nop()
                    eng.nop()
                eng.nop()
            if leave:
                leave()

        def round_of(i, b):
            return (i - b) * 8

        with nc.Block() as block:
            @block.sync
            def _(sp):
                def turn(e, slot, first=False):
                    if not first:
                        sp.wait_ge(entered, e - 1)
                    load_expert(sp, a, wexp, e, slot, slot_in[slot])

                def land(e, slot, round_):
                    sp.wait_ge(slot_in[slot], 48 * round_ + 48)
                    sp.sem_inc(w_ok, 1)

                turn(2, 2, True)
                land(0, 0, 0)
                land(1, 1, 0)
                turn(3, 3, True)
                land(2, 2, 0)
                with sp.Fori(1, E // RING) as r:
                    for j in range(RING):
                        turn(r * RING + j, j)
                        land(r * RING + j - 1, (j - 1) % RING, r if j else r - 1)
                land(E - 1, RING - 1, E // RING - 1)

            @block.gpsimd
            def _(pool):
                pool.memset(xg[:, :, XW:XW + 1], 0.0).then_inc(pad_ok, 1)
                pool.memset(none[:], 0.0).then_inc(pad_ok, 1)
                pool.wait_ge(pad_ok, 2)
                for c in range(2):
                    pool.dma_start(acc_d[ROW0 + TT:, c * (D // 2):(c + 1) * (D // 2)], none[:]).then_inc(added, 16)

                def gather(j, b):
                    pool.wait_ge(ix_ok, j + 1)
                    pool.sem_inc(passed, 1)
                    pool.indirect_dma_start(out=xg[:, b, 0:XW], out_offset=None, in_=xe_d,
                                            in_offset=bass.IndirectOffsetOnAxis(ap=ix[b][:, 0:1], axis=0)).then_inc(gat[b], 16)

                gather(0, 0)
                gather(1, 1)
                pool.wait_ge(x_tp, 1)
                pool.wait_ge(wc_ok, 1)
                gather(2, 0)

                def block_of(i, b):
                    pool.wait_ge(x_tp, i + 2)
                    pool.wait_ge(wc_ok, i + 2)
                    gather(i + 3, 1 - b)
                    pool.wait_ge(ob_ok, 2 * i + 4)
                    pool.wait_ge(ixs_ok, i + 1)
                    pool.wait_ge(added, 16 * i + 32)
                    pool.sem_inc(passed, 1)
                    pool.indirect_dma_start(out=acc_d, out_offset=bass.IndirectOffsetOnAxis(ap=ixs[b][:, 0:1], axis=0),
                                            in_=ob[:, b, :], in_offset=None, compute_op=ALU.add).then_inc(added, 16)

                blocks(pool, block_of)
                n = pool.value_load(total[0:1, 0:1], min_val=E, max_val=ITEMS)
                pool.wait_ge(added, 16 * n + 32)
                pool.wait_ge(gat[0], 16 * ((n + 4) // 2))
                pool.wait_ge(gat[1], 16 * ((n + 3) // 2))

            @block.tensor
            def _(pe):
                def index(j, b, later=True):
                    pe.wait_ge(oh_ok, j + 1)
                    if later:
                        pe.wait_ge(list_ok, j - 1)
                    for t in range(TILES):
                        last = pe.matmul(banks[6 + b][:, 0:2], oh[:, b, t, :], tok[:, t, :], start=(t == 0),
                                         stop=(t == TILES - 1))
                    last.then_inc(ix_ps, 1)

                def turn(j, b, landed):
                    pe.wait_ge(gat[b], landed)
                    if j is not 0:
                        pe.wait_ge(xT_ok, 2 * j)
                    for k in range(KD):
                        last = pe.transpose(banks[1 + k // 4][:, (k % 4) * P:(k % 4 + 1) * P], xg[:, b, k * P:(k + 1) * P],
                                            ident[:])
                    last.then_inc(x_tp, 1)

                def up(j, b, e, c):
                    slot = e & (RING - 1)

                    def part(k):
                        return pe.matmul(banks[0][:], xT[:, b, k, :],
                                         wexp[:, bass.ds(slot, 1), k, :].rearrange("p a n -> p (a n)"),
                                         start=(k == 0), stop=(k == KD - 1))

                    pe.wait_ge(xT_ok, 2 * j + 2)
                    with pe.If(c < 1):
                        pe.wait_ge(w_ok, e + 1)
                        part(0).then_inc(entered, 1)
                    with pe.Else():
                        part(0)
                    for k in range(1, KD):
                        last = part(k)
                    last.then_inc(gu_ps, 1)

                index(0, 0, False)
                index(1, 1, False)
                turn(0, 0, 16)
                index(2, 0)
                turn(1, 1, 16)
                index(3, 1)
                pe.sem_inc(ob_ok, 2)
                up(0, 0, entry(pe, 0, 0, E), entry(pe, 0, 1, (TILES - 1) * P))

                def block_of(i, b):
                    e = entry(pe, i, 0, E)
                    pe.wait_ge(h_ok, i + 1)
                    for f in range(FF // P):
                        last = pe.transpose(banks[3][:, f * P:(f + 1) * P], hh[:, f * P:(f + 1) * P], ident[:])
                    last.then_inc(h_tp, 1)
                    up(i + 1, 1 - b, entry(pe, i + 1, 0, E), entry(pe, i + 1, 1, (TILES - 1) * P))
                    index(i + 4, b)
                    turn(i + 2, b, round_of(i, b) + 32)
                    slot = e & (RING - 1)
                    pe.wait_ge(hT_ok, i + 1)
                    pe.wait_ge(ob_ok, 2 * i + 2)
                    for half in range(2):
                        for f in range(FF // P):
                            last = pe.matmul(banks[4 + half][:], hT[:, f, :],
                                             wexp[:, bass.ds(slot, 1), KD + 2 * f + half, :].rearrange("p a n -> p (a n)"),
                                             start=(f == 0), stop=(f == FF // P - 1))
                    last.then_inc(dn_ps, 1)

                blocks(pe, block_of)

            @block.scalar
            def _(act):
                def take(j, b):
                    act.wait_ge(x_tp, j + 1)
                    act.wait_ge(gu_ps, j - 1) if j is not 0 and j is not 1 else None
                    act.activation(xT[:, b, 0:4, :].rearrange("p k n -> p (k n)"), banks[1][:], ACT.Copy).then_inc(xT_ok, 1)

                def gate(j):
                    act.wait_ge(gu_ps, j + 1)
                    act.activation(sg[:], banks[0][:, 0:FF], ACT.Silu).then_inc(sg_ok, 1)

                take(0, 0)
                take(1, 1)
                gate(0)

                def block_of(i, b):
                    act.wait_ge(h_tp, i + 1)
                    act.activation(hT[:].rearrange("p f n -> p (f n)"), banks[3][:, 0:FF], ACT.Copy).then_inc(hT_ok, 1)
                    gate(i + 1)
                    take(i + 2, b)
                    act.wait_ge(dn_ps, i + 1)
                    act.wait_ge(ixs_ok, i + 1)
                    act.activation(ob[:, b, 0:512], banks[4][:], ACT.Copy, scale=wcol[:, b:b + 1]).then_inc(ob_ok, 1)

                blocks(act, block_of)

            @block.vector
            def _(dve):
                s = Steps(dve, dve6)

                def place(j, b):
                    e = entry(dve, j, 0, E)
                    c = entry(dve, j, 1, (TILES - 1) * P)
                    dve.tensor_tensor(oh[:, b, :, :], iota[:, bass.ds(c, P)].unsqueeze(1).to_broadcast([P, TILES, P]),
                                      posm[:, bass.ds(e, 1), :].rearrange("p a t -> p (a t)").unsqueeze(2).to_broadcast([P, TILES, P]),
                                      ALU.is_equal).then_inc(oh_ok, 1)

                def index(j, b):
                    dve.wait_ge(ix_ps, j + 1)
                    s.link(dve.tensor_copy(ixf[:, 0:2], banks[6 + b][:, 0:2]))
                    s.link(dve.tensor_tensor(ixf[:, 2:3], ixf[:, 0:1], ixf[:, 1:2], ALU.add))
                    s.link(dve.scalar_tensor_tensor(out=ixf[:, 3:4], in0=ixf[:, 2:3], scalar=0.0, in1=idle[:], op0=ALU.is_equal,
                                                    op1=ALU.mult))
                    dve.tensor_tensor(lists[:, bass.ds(j & (LISTS - 1), 1)], ixf[:, 2:3], ixf[:, 3:4], ALU.add).then_inc(list_ok, 1)

                def take(j, b):
                    dve.wait_ge(x_tp, j + 1)
                    dve.tensor_copy(xT[:, b, 4:8, :].rearrange("p k n -> p (k n)"), banks[2][:]).then_inc(xT_ok, 1)

                def weight(j, b, e, landed):
                    dve.wait_ge(gat[b], landed)
                    dve.tensor_copy(wcol[:, b:b + 1], xg[:, b, bass.ds(e + D, 1)]).then_inc(wc_ok, 1)

                def gate(j):
                    dve.wait_ge(sg_ok, j + 1)
                    dve.tensor_tensor(hh[:], sg[:], banks[0][:, FF:], ALU.mult).then_inc(h_ok, 1)

                def to_gather(j, b):
                    dve.wait_ge(list_ok, j + 1)
                    dve.tensor_copy(ix[b][:], lists[:, bass.ds(j & (LISTS - 1), 1)]).then_inc(ix_ok, 1)

                def to_add(j, b):
                    dve.tensor_copy(ixs[b][:], lists[:, bass.ds(j & (LISTS - 1), 1)]).then_inc(ixs_ok, 1)

                dve.wait_ge(pad_ok, 2)
                for j in range(2):
                    place(j, j)
                for j in range(2):
                    index(j, j)
                    to_gather(j, j)
                take(0, 0)
                weight(0, 0, entry(dve, 0, 0, E), 16)
                place(2, 0)
                index(2, 0)
                to_gather(2, 0)
                place(3, 1)
                take(1, 1)
                weight(1, 1, entry(dve, 1, 0, E), 16)
                index(3, 1)
                gate(0)

                def block_of(i, b):
                    dve.wait_ge(gat[1 - b], round_of(i, b) + 16 + 16 * b)
                    to_gather(i + 3, 1 - b)
                    place(i + 4, b)
                    gate(i + 1)
                    dve.wait_ge(gu_ps, i + 2)
                    take(i + 2, b)
                    dve.wait_ge(added, 16 * i + 16)
                    to_add(i, b)
                    index(i + 4, b)
                    dve.wait_ge(dn_ps, i + 1)
                    dve.tensor_scalar(ob[:, b, 512:], banks[5][:], wcol[:, b:b + 1], None, ALU.mult).then_inc(ob_ok, 1)
                    dve.wait_ge(ob_ok, 2 * i + 4)
                    weight(i + 2, b, entry(dve, i + 2, 0, E), round_of(i, b) + 32)

                blocks(dve, block_of, lambda it: s.enter(it, 2 * 3), lambda: s.leave(ITEMS // 2))


def final(nc, a, o, sb, sem, eps, mod_d, x2_d, acc_d):
    with ExitStack() as ctx:
        def tile(name, shape, dt=F32):
            return sb(name, shape, dt, ctx)

        g2 = tile("g2", [P, D])
        g2s = tile("g2s", [NS, D])
        fg = tile("fg", [P, D])
        xx = tile("xx", [P, 4, D])
        aa = tile("aa", [P, 4, D])
        yy = tile("yy", [P, 2, D])
        sqj = tile("sqf", [P, D])
        st = tile("stf", [P, 4])
        c_in, sum_ok, sq_ok, sd_ok, y_ok = (sem("s7" + n) for n in "c sum sq sd y".split())
        t_in = [sem(f"s7i{j}") for j in range(4)]
        out = [sem(f"s7o{j}") for j in range(2)]
        dve7 = sem("dve7")
        y_p = o["y_prompt"].rearrange("b t d -> (b t) d")
        y_s = o["y_sample"].rearrange("b t d -> (b t) d")
        with nc.Block() as block:
            @block.sync
            def _(sp):
                sp.dma_start(g2[:], mod_d[NS:NS + 1, 5 * D:].to_broadcast([P, D])).then_inc(c_in, 16)
                sp.dma_start(g2s[:], mod_d[0:NS, 5 * D:]).then_inc(c_in, 16)
                sp.dma_start(fg[:], a["final_norm_g"].rearrange("(a n) -> a n", a=1).to_broadcast([P, D])).then_inc(c_in, 16)
                for t in range(TILES):
                    r = rows_of(t)
                    if t >= 4:
                        sp.wait_ge(y_ok, t - 3)
                    sp.dma_start(aa[0:r, t % 4, :], acc_d[ROW0 + t * P:ROW0 + t * P + r, :]).then_inc(t_in[t % 4], 16)
                    sp.dma_start(xx[0:r, t % 4, :], x2_d[t * P:t * P + r, :]).then_inc(t_in[t % 4], 16)

            @block.scalar
            def _(act):
                for t in range(TILES):
                    r = rows_of(t)
                    act.wait_ge(sum_ok, t + 1)
                    if t:
                        act.wait_ge(y_ok, t)
                    act.activation(sqj[0:r, :], aa[0:r, t % 4, :], ACT.Square, accum_out=st[0:r, 0:1]).then_inc(sq_ok, 1)
                    act.wait_ge(sq_ok, t + 1)
                    act.activation(st[0:r, 1:2], st[0:r, 0:1], ACT.Sqrt, scale=1.0 / D, bias=eps[0:r, 0:1]).then_inc(sd_ok, 1)

            @block.gpsimd
            def _(pool):
                for t in range(TILES):
                    r = rows_of(t)
                    pool.wait_ge(y_ok, t + 1)
                    pool.dma_start(y_p[t * P:(t + 1) * P, :] if t < TILES - 1 else y_s, yy[0:r, t % 2, :]).then_inc(out[t % 2], 16)
                for b in range(2):
                    pool.wait_ge(out[b], 16 * ((TILES + 1 - b) // 2))

            @block.vector
            def _(dve):
                s = Steps(dve, dve7)
                dve.wait_ge(c_in, 48)
                for t in range(TILES):
                    r = rows_of(t)
                    dve.wait_ge(t_in[t % 4], 32 * (t // 4 + 1))
                    acc = aa[0:r, t % 4, :]
                    s.link(dve.tensor_tensor(acc, acc, (g2 if t < TILES - 1 else g2s)[0:r, :], ALU.mult))
                    dve.tensor_tensor(acc, acc, xx[0:r, t % 4, :], ALU.add).then_inc(sum_ok, 1)
                    dve.wait_ge(sd_ok, t + 1)
                    s.link(dve.reciprocal(st[0:r, 2:3], st[0:r, 1:2]))
                    if t >= 2:
                        dve.wait_ge(out[t % 2], 16 * (t // 2))
                    dve.scalar_tensor_tensor(out=yy[0:r, t % 2, :], in0=acc, scalar=st[0:r, 2:3], in1=fg[0:r, :],
                                             op0=ALU.mult, op1=ALU.mult).then_inc(y_ok, 1)


_INS = ["x_prompt", "x_sample", "state_hgrn", "state_conv", "c_prompt", "c_sample", "w_ada", "b_ada", "norm_mix_g",
        "norm_ffn_g", "w_in", "lb_logits", "hgrn_norm_g", "conv_w", "conv_b", "w_out_hgrn", "w_out_conv", "w_o",
        "w_router", "router_bias", "w_exp_gate", "w_exp_up", "w_exp_down", "w_sh_gate", "w_sh_up", "w_sh_down",
        "final_norm_g"]
_OUTS = [("y_prompt", (1, T, D)), ("y_sample", (NS, 1, D)), ("hgrn_prompt", (1, 1, H, HK, HK)),
         ("conv_prompt", (1, 1, 2, W)), ("hgrn_sample", (1, NS, H, HK, HK)), ("conv_sample", (1, NS, 2, W))]


def kernel(**inputs):
    import concourse.bacc as bacc
    from concourse.bass_utils import run_bass_kernel_spmd

    nc = bacc.Bacc("TRN2", target_bir_lowering=False, num_devices=1)
    arrays, a, o = {}, {}, {}
    for name in _INS:
        arrays["in_" + name] = np.ascontiguousarray(inputs[name])
        a[name] = nc.dram_tensor("in_" + name, arrays["in_" + name].shape, F32, kind="ExternalInput").ap()
    for name, shape in _OUTS:
        o[name] = nc.dram_tensor("out_" + name, shape, F32, kind="ExternalOutput").ap()
    layer(nc, a, o)
    r = run_bass_kernel_spmd(nc, [arrays], core_ids=[0])
    return tuple(r.results[0]["out_" + name] for name, _ in _OUTS)
```
